# Optimizing a Trainium2 kernel written in Bass

```python
import math
import jax, jax.numpy as jnp
from jax import lax
import numpy as np

D_MODEL = 2048
BATCH = 1
SEQ = 256
DEPTH = 2

CHUNK = 64
Q_BLOCK = 128
ROPE_THETA = 10000.0
NORM_EPS = 1e-6
HEAD_NORM_EPS = 1e-5
NEG_INF = -1e30
N_EVEN = (DEPTH + 1) // 2
N_ODD = DEPTH // 2

A_WIDTH = D_MODEL // 2
A_HD = 64
A_HEADS = A_WIDTH // A_HD
A_KV = max(1, A_HEADS // 8)
A_GROUP = A_HEADS // A_KV
SWA_WINDOW = 128
SWA_CHUNKS = SWA_WINDOW // CHUNK

B_WIDTH = D_MODEL - A_WIDTH
B_HD = 128
B_HEADS = B_WIDTH // (2 * B_HD)

C_HEADS = 4
C_DK = D_MODEL // 2 // C_HEADS
C_DV = D_MODEL // C_HEADS
C_RANK = 16
GATE_TAU = 16.0

AB_SIZES = (A_HEADS * A_HD, A_KV * A_HD, A_KV * A_HD, A_WIDTH,
            B_HEADS * 2 * B_HD, B_HEADS * 2 * B_HD, B_WIDTH, B_WIDTH)
AB_IN = sum(AB_SIZES)
AB_MIX = A_WIDTH + B_WIDTH
C_SIZES = (C_HEADS * C_DK, C_HEADS * C_DK, C_HEADS * C_DV, C_HEADS * C_DV, C_RANK)
C_IN = sum(C_SIZES)
C_MIX = C_HEADS * C_DV

kernel_name = "chunk_causal_hybrid_swa_diff_gla"

def _split(t, sizes):
    idx = [int(i) for i in np.cumsum(sizes)[:-1]]
    return jnp.split(t, idx, axis=-1)

def _rms(x, g, eps):
    xf = x.astype(jnp.float32)
    y = xf * lax.rsqrt(jnp.mean(xf * xf, axis=-1, keepdims=True) + eps)
    return (y * g.astype(jnp.float32)).astype(x.dtype)

def _rope(x, pos):
    d = x.shape[-1]
    half = d // 2
    inv = ROPE_THETA ** (-jnp.arange(half, dtype=jnp.float32) / half)
    ang = pos.astype(jnp.float32)[:, None] * inv[None, :]
    shape = (1, x.shape[1]) + (1,) * (x.ndim - 3) + (half,)
    cos = jnp.cos(ang).reshape(shape)
    sin = jnp.sin(ang).reshape(shape)
    x1 = x[..., :half].astype(jnp.float32)
    x2 = x[..., half:].astype(jnp.float32)
    return jnp.concatenate([x1 * cos - x2 * sin, x2 * cos + x1 * sin], axis=-1).astype(x.dtype)

def _band(t):
    n_c = t.shape[1]
    parts = []
    for j in range(SWA_CHUNKS - 1, -1, -1):
        pad = [(0, 0)] * t.ndim
        pad[1] = (j, 0)
        parts.append(jnp.pad(t, pad)[:, :n_c])
    return jnp.concatenate(parts, axis=2)

def sliding_window_sink_attention(q, k, v, sinks):
    bn, s_len, _, d = q.shape
    n_c = s_len // CHUNK
    qc = q.reshape(bn, n_c, CHUNK, A_KV, A_GROUP, d)
    kb = _band(k.reshape(bn, n_c, CHUNK, A_KV, d))
    vb = _band(v.reshape(bn, n_c, CHUNK, A_KV, d))
    s = jnp.einsum('bclkgd,bcmkd->bckglm', qc, kb).astype(jnp.float32) * (d ** -0.5)
    shifts = np.arange(SWA_CHUNKS - 1, -1, -1)
    valid = jnp.arange(n_c)[:, None] >= shifts[None, :]
    valid = jnp.repeat(valid, CHUNK, axis=1)
    s = jnp.where(valid[None, :, None, None, None, :], s, NEG_INF)
    sink = sinks.astype(jnp.float32).reshape(A_KV, A_GROUP)[None, None, :, :, None, None]
    sink = jnp.broadcast_to(sink, s.shape[:-1] + (1,))
    p = jax.nn.softmax(jnp.concatenate([s, sink], axis=-1), axis=-1)[..., :-1]
    o = jnp.einsum('bckglm,bcmkd->bclkgd', p.astype(v.dtype), vb)
    return o.reshape(bn, s_len, A_HEADS * d)

def differential_attention(q, k, v, lam, head_gain, lambda_init):
    bn, s_len, h, _, d = q.shape
    n_qb = s_len // Q_BLOCK
    k_chunk = jnp.arange(s_len) // CHUNK
    scale = d ** -0.5

    def block(args):
        qb, qi = args
        s = jnp.einsum('bqhcd,bkhcd->bhcqk', qb, k).astype(jnp.float32) * scale
        q_chunk = (qi * Q_BLOCK + jnp.arange(Q_BLOCK)) // CHUNK
        s = jnp.where(k_chunk[None, :] <= q_chunk[:, None], s, NEG_INF)
        p = jax.nn.softmax(s, axis=-1)
        w = p[:, :, 0] - lam * p[:, :, 1]
        return jnp.einsum('bhqk,bkhv->bqhv', w.astype(v.dtype), v)

    qs = jnp.swapaxes(q.reshape(bn, n_qb, Q_BLOCK, h, 2, d), 0, 1)
    o = lax.map(block, (qs, jnp.arange(n_qb)))
    o = jnp.swapaxes(o, 0, 1).reshape(bn, s_len, h, 2 * d)
    o = _rms(o, head_gain, HEAD_NORM_EPS) * (1.0 - lambda_init)
    return o.reshape(bn, s_len, h * 2 * d)

def hybrid_attention_layer(hn, w_in, w_out, sinks, lq1, lk1, lq2, lk2, head_gain, lambda_init, pos):
    bn, s_len, _ = hn.shape
    aq, ak, av, ag, bq, bk, bv, bg = _split(hn @ w_in, AB_SIZES)
    aq = _rope(aq.reshape(bn, s_len, A_HEADS, A_HD), pos)
    ak = _rope(ak.reshape(bn, s_len, A_KV, A_HD), pos)
    av = av.reshape(bn, s_len, A_KV, A_HD)
    a_out = sliding_window_sink_attention(aq, ak, av, sinks)
    bq = _rope(bq.reshape(bn, s_len, B_HEADS, 2, B_HD), pos)
    bk = _rope(bk.reshape(bn, s_len, B_HEADS, 2, B_HD), pos)
    bv = bv.reshape(bn, s_len, B_HEADS, 2 * B_HD)
    lam = (jnp.exp(jnp.sum(lq1.astype(jnp.float32) * lk1.astype(jnp.float32)))
           - jnp.exp(jnp.sum(lq2.astype(jnp.float32) * lk2.astype(jnp.float32)))
           + lambda_init)
    b_out = differential_attention(bq, bk, bv, lam, head_gain, lambda_init)
    y = jnp.concatenate([a_out * jax.nn.silu(ag), b_out * jax.nn.silu(bg)], axis=-1)
    return y @ w_out

def _gla_chunked(q, k, v, g):
    bn, s_len, h, dk = q.shape
    dv = v.shape[-1]
    n_c = s_len // CHUNK
    q = q.reshape(bn, n_c, CHUNK, h, dk)
    k = k.reshape(bn, n_c, CHUNK, h, dk)
    v = v.reshape(bn, n_c, CHUNK, h, dv)
    b = jnp.cumsum(g.reshape(bn, n_c, CHUNK, h, dk), axis=2)
    b_last = b[:, :, -1:]
    q_e = q * jnp.exp(b)
    k_e = k * jnp.exp(-b)
    k_t = k * jnp.exp(b_last - b)
    causal = jnp.tril(jnp.ones((CHUNK, CHUNK), dtype=bool))
    att = jnp.einsum('bclhd,bcmhd->bchlm', q_e, k_e)
    att = jnp.where(causal, att, 0.0)
    o_intra = jnp.einsum('bchlm,bcmhv->bclhv', att, v)
    decay = jnp.exp(b_last[:, :, 0])

    def step(state, inp):
        qe, kt, vc, dec = inp
        o = jnp.einsum('blhd,bhdv->blhv', qe, state)
        state = state * dec[..., None] + jnp.einsum('blhd,blhv->bhdv', kt, vc)
        return state, o

    s0 = jnp.zeros((bn, h, dk, dv), jnp.float32)
    xs = (jnp.moveaxis(q_e, 1, 0), jnp.moveaxis(k_t, 1, 0),
          jnp.moveaxis(v, 1, 0), jnp.moveaxis(decay, 1, 0))
    _, o_inter = lax.scan(step, s0, xs)
    o = o_intra + jnp.moveaxis(o_inter, 0, 1)
    return o.reshape(bn, s_len, h, dv)

def gla_layer(hn, w_in, w_gate2, gate_b, head_gain, w_out):
    bn, s_len, _ = hn.shape
    q, k, v, r, lr = _split(hn @ w_in, C_SIZES)
    z = lr @ w_gate2 + gate_b
    g = jax.nn.log_sigmoid(z.astype(jnp.float32)) / GATE_TAU
    q = q.reshape(bn, s_len, C_HEADS, C_DK).astype(jnp.float32) * (C_DK ** -0.5)
    k = k.reshape(bn, s_len, C_HEADS, C_DK).astype(jnp.float32)
    v = v.reshape(bn, s_len, C_HEADS, C_DV).astype(jnp.float32)
    g = g.reshape(bn, s_len, C_HEADS, C_DK)
    o = _gla_chunked(q, k, v, g).astype(hn.dtype)
    o = _rms(o, head_gain, HEAD_NORM_EPS).reshape(bn, s_len, C_MIX)
    return (o * jax.nn.silu(r)) @ w_out

def setup_inputs(seed: int = 0) -> dict:
    key = jax.random.key(seed)
    ks = jax.random.split(key, 17)
    f32 = jnp.float32
    nrm = lambda k, shape, s: jax.random.normal(k, shape, f32) * s
    return {
        "x": nrm(ks[0], (BATCH, SEQ, D_MODEL), 1.0),
        "norm_g": 1.0 + nrm(ks[1], (DEPTH, D_MODEL), 0.02),
        "final_g": 1.0 + nrm(ks[2], (D_MODEL,), 0.02),
        "ab_w_in": nrm(ks[3], (N_EVEN, D_MODEL, AB_IN), D_MODEL ** -0.5),
        "ab_w_out": nrm(ks[4], (N_EVEN, AB_MIX, D_MODEL), AB_MIX ** -0.5),
        "a_sinks": nrm(ks[5], (N_EVEN, A_HEADS), 0.5),
        "b_lq1": nrm(ks[6], (N_EVEN, B_HD), 0.1),
        "b_lk1": nrm(ks[7], (N_EVEN, B_HD), 0.1),
        "b_lq2": nrm(ks[8], (N_EVEN, B_HD), 0.1),
        "b_lk2": nrm(ks[9], (N_EVEN, B_HD), 0.1),
        "b_head_g": 1.0 + nrm(ks[10], (N_EVEN, 2 * B_HD), 0.02),
        "c_w_in": nrm(ks[11], (N_ODD, D_MODEL, C_IN), D_MODEL ** -0.5),
        "c_w_gate2": nrm(ks[12], (N_ODD, C_RANK, C_HEADS * C_DK), C_RANK ** -0.5),
        "c_gate_b": nrm(ks[13], (N_ODD, C_HEADS * C_DK), 0.1),
        "c_head_g": 1.0 + nrm(ks[14], (N_ODD, C_DV), 0.02),
        "c_w_out": nrm(ks[15], (N_ODD, C_MIX, D_MODEL), C_MIX ** -0.5),
    }

def reference(x, norm_g, final_g, ab_w_in, ab_w_out, a_sinks, b_lq1, b_lk1, b_lq2, b_lk2,
              b_head_g, c_w_in, c_w_gate2, c_gate_b, c_head_g, c_w_out):
    pos = jnp.arange(x.shape[1])
    h = x
    for l in range(DEPTH):
        hn = _rms(h, norm_g[l], NORM_EPS)
        i = l // 2
        if l % 2 == 0:
            lambda_init = 0.8 - 0.6 * math.exp(-0.3 * l)
            y = hybrid_attention_layer(hn, ab_w_in[i], ab_w_out[i], a_sinks[i],
                                       b_lq1[i], b_lk1[i], b_lq2[i], b_lk2[i],
                                       b_head_g[i], lambda_init, pos)
        else:
            y = gla_layer(hn, c_w_in[i], c_w_gate2[i], c_gate_b[i], c_head_g[i], c_w_out[i])
        h = h + y
    return _rms(h, final_g, NORM_EPS)


_drawn_inputs = setup_inputs


def setup_inputs(seed=0):
    import zlib

    import numpy as np

    out = dict(_drawn_inputs(seed))
    spreads = {}
    factors = {'final_g': 2.769, 'a_sinks': 8.0, 'b_lk2': 3.085, 'b_head_g': 6.511, 'c_head_g': 6.122}
    for name, (base, spread) in spreads.items():
        noise = np.random.default_rng([zlib.crc32(name.encode()), seed]).standard_normal(out[name].shape)
        drawn = base * np.exp(spread * noise) if base else spread * noise
        out[name] = __import__('jax').numpy.asarray(drawn.astype(out[name].dtype))
    for name, factor in factors.items():
        out[name] = (out[name] * factor).astype(out[name].dtype)
    return out
```

```python
import math
from contextlib import ExitStack

import numpy as np

import concourse.bass as bass
from concourse import mybir

F32 = mybir.dt.float32
F32R = mybir.dt.float32r
U32 = mybir.dt.uint32
ALU = mybir.AluOpType
ACT = mybir.ActivationFunctionType
AX_X = mybir.AxisListType.X

P = 128
D = 2048
S = 256
NT = S // P
KT = D // P
CHUNK = 64
A_HD, A_HEADS, A_KV = 64, 16, 2
A_GROUP = A_HEADS // A_KV
B_HD, B_HEADS = 128, 4
B_MAPS = 2 * B_HEADS
C_HEADS, C_DK, C_DV, C_RANK = 4, 256, 512, 16
C_DKS = C_HEADS * C_DK
GATE_TAU = 16.0
THETA = 10000.0
NEG = -1e30
NORM_EPS, HEAD_EPS = 1e-6, 1e-5
LAMBDA_INIT = 0.8 - 0.6 * math.exp(-0.3 * 0)

N = 512
HALVES = 8
UNITS = 4
SPLIT_RING = 4

AQ, AK = 0, A_HEADS * A_HD
AG = AK + 2 * A_KV * A_HD
BQ = AG + D // 2
BK, BV, BG = BQ + 1024, BQ + 2048, BQ + 3072
CQ, CK, CV, CR = 0, C_DKS, 2 * C_DKS, 2 * C_DKS + C_HEADS * C_DV
CLR = CR + C_HEADS * C_DV

BLOCKS = [("kv", 0, "ab_in", AK, 2 * A_KV * A_HD)]
BLOCKS += [(k, c, "ab_in", at + N * c, N) for k, at in (("aq", AQ), ("bq", BQ), ("bk", BK), ("bv", BV), ("ag", AG), ("bg", BG)) for c in range(2)]
BLOCKS += [("out0", c, "ab_out", N * c, N) for c in range(4)]
BLOCKS += [("v", c, "c_in", CV + N * c, N) for c in range(4)]
BLOCKS += [(k, c, "c_in", at + N * c, N) for k, at in (("q", CQ), ("k", CK)) for c in range(2)]
BLOCKS += [("r", c, "c_in", CR + N * c, N) for c in range(4)]
BLOCKS += [("out1", c, "c_out", N * c, N) for c in range(4)]
NB = len(BLOCKS)
POS = {(k, c): p for p, (k, c, _, _, _) in enumerate(BLOCKS, 1)}

_widths = [("ident", P), ("cosA", NT * 32), ("sinA", NT * 32), ("cosB", NT * 64), ("sinB", NT * 64),
           ("mask", 5 * CHUNK), ("tri", P), ("cum64", P), ("rev64", P), ("rev128", CHUNK), ("tail", P)]
CONST_AT, CONST_W = {}, 0
for _n, _w in _widths:
    CONST_AT[_n] = (CONST_W, CONST_W + _w)
    CONST_W += _w


def constants():
    t = np.zeros((P, CONST_W), np.float32)

    def put(name, a):
        lo, hi = CONST_AT[name]
        t[:, lo:hi] = a

    put("ident", np.eye(P))
    for name, half in (("A", A_HD // 2), ("B", B_HD // 2)):
        inv = np.float32(THETA) ** (-np.arange(half, dtype=np.float32) / np.float32(half))
        ang = np.arange(S, dtype=np.float32)[:, None] * inv[None, :].astype(np.float32)
        for f, fn in (("cos", np.cos), ("sin", np.sin)):
            put(f + name, fn(ang).reshape(NT, P, half).transpose(1, 0, 2).reshape(P, -1))
    row = np.arange(P)[:, None]
    col = np.arange(P)[None, :]
    m = np.zeros((P, 5, CHUNK), np.float32)
    m[CHUNK:, 0] = NEG
    m[:CHUNK, 4] = NEG
    put("mask", m.reshape(P, -1))
    put("tri", row <= col)
    same = row // CHUNK == col // CHUNK
    put("cum64", (row <= col) & same)
    put("rev64", (row > col) & same)
    put("rev128", (row > col)[:, :CHUNK])
    put("tail", np.where(col < CHUNK, (row > col) & same, row <= col))
    return t


TASKS = []


def _plan():
    add = TASKS.append
    for kt in range(KT):
        add((f"x{kt}", "dve"))
    add(("akT", "act"))
    for g in range(4):
        add((f"aqT{g}", "act"))
        if g:
            for h in range(4 * g - 4, 4 * g):
                add((f"SA{h}", "dve"))
    for g in range(4):
        add((f"bqT{g}", "act"))
        if g == 0:
            for h in range(12, 16):
                add((f"SA{h}", "dve"))
    for g in range(4):
        add((f"bkT{g}", "act"))
    for m in range(B_MAPS):
        add((f"SB{m}", "dve"))
    for h in range(A_HEADS):
        add((f"PA{h}", "act" if h % 2 else "dve"))
    for h in range(B_HEADS):
        add((f"PB{h}", "act" if h % 2 else "dve"))
        if h:
            add((f"OB{h - 1}", "dve"))
    add((f"OB{B_HEADS - 1}", "dve"))
    for kt in range(KT):
        add((f"y{kt}", "dve"))
    for kt in range(KT):
        add((f"h{kt}", "dve"))
    add(("lr", "dve"))
    for t in range(NT):
        for c in range(2):
            add((f"z{t}{c}", "dve"))
    for name in ("cum0", "rev0", "far0", "cum1", "tail1"):
        for c in range(2):
            add((f"{name}{c}", "act"))
    for g in range(4):
        add((f"qeT{g}", "act"))
    for g in range(4):
        add((f"keT{g}", "dve"))
    for g in range(2):
        add((f"a0T{g}", "act"))
    for g in range(2):
        add((f"w1T{g}", "dve"))
    add(("k0T", "act"))
    for h in range(C_HEADS):
        add((f"SC{h}", "dve"))
    for h in range(C_HEADS):
        for t in range(NT):
            add((f"OC{h}{t}", "dve"))
    for kt in range(KT):
        add((f"u{kt}", "dve"))


_plan()
TASK = {name: k for k, (name, _) in enumerate(TASKS)}
BANKS = 4


def freed(k):
    return TASKS[k][1], sum(e == TASKS[k][1] for _, e in TASKS[:k + 1])


class Steps:

    def __init__(self, eng, sem):
        self.eng, self.sem, self.n = eng, sem, 0

    def did(self, ins):
        ins.then_inc(self.sem, 1)
        self.n += 1
        return self.n

    def wait(self, n=None):
        self.eng.wait_ge(self.sem, self.n if n is None else n)


def build(nc, x, consts, gains, bhg, chg, final_g, w_ab_in, w_ab_out, w_c_in, w_c_out, sinks, lams,
          gate2, gate_b, out):
    W = {"ab_in": w_ab_in, "ab_out": w_ab_out, "c_in": w_c_in, "c_out": w_c_out}
    with ExitStack() as ctx:
        def sb(name, shape, dt=F32):
            return ctx.enter_context(nc.sbuf_tensor(name, shape, dt))

        def sem(name):
            return ctx.enter_context(nc.semaphore(name))

        xres = sb("xres", [P, NT, D])
        xTh = sb("xTh", [P, KT, S], F32R)
        xTl = sb("xTl", [P, KT, S], F32R)
        raw = sb("raw", [P, UNITS, 4, N])
        wh = sb("wh", [P, SPLIT_RING, 2, N], F32R)
        wl = sb("wl", [P, SPLIT_RING, 2, N], F32R)
        cst = sb("cst", [P, CONST_W])
        rope = sb("rope", [P, 384])
        gain = sb("gain", [P, 4, KT])
        hg = sb("hg", [P, 2 + 4])
        sink = sb("sink", [P, A_HEADS])
        small = sb("small", [P, 400])
        tA = sb("tA", [P, NT, N])
        tB = sb("tB", [P, N])
        tC = sb("tC", [P, N])
        lrh = sb("lrh", [P, KT * C_RANK + 64], F32R)
        lrl = sb("lrl", [P, KT * C_RANK + 64], F32R)
        arena = sb("arena", [P, 18816])

        def area(at, *shape):
            a = arena[:, at:at + int(np.prod(shape))]
            if len(shape) == 1:
                return a
            names = "abcd"[:len(shape)]
            return a.rearrange(f"p ({' '.join(names)}) -> p {' '.join(names)}", **dict(zip(names[1:], shape[1:])))

        aq = area(0, NT, 1024)
        bqT = area(0, B_MAPS, S)
        bq = area(2048, NT, 1024)
        bk = area(4096, NT, 1024)
        pB = area(2048, B_MAPS, 384)
        bv = area(6144, NT, 1024)
        ya = area(8192, NT, 1024)
        aqT = area(10240, 8, S)
        bkT = area(10240, B_MAPS, S)
        pT = area(10240, 4, 384)
        pA = area(12288, A_HEADS, 320)
        yb = area(12288, NT, 1024)
        junkB = area(16384, S)
        akT = area(17408, A_KV, S)
        av = area(17920, 3, P)
        akr = area(18304, NT, A_KV, 2, A_HD)
        lam_in = area(6144, 4, B_HD)
        junk0 = area(12288, D)
        junkO = area(18304, N)
        v = area(0, NT, D)
        zs = area(4096, NT, C_DKS)
        gs = area(6144, NT, C_DKS)
        g2 = area(8192, C_DKS)
        gb = area(9216, C_DKS)
        lrw = area(10240, KT * C_RANK)
        lrT = area(10496, S)
        qeT = area(4096, 8, S)
        keT = area(6144, 8, S)
        a0T = area(8192, 8, P)
        kkT = area(9216, 8, P)
        w1T = area(10240, 8, P)
        qe = area(11264, NT, C_DKS)
        ke = area(13312, NT, C_DKS)
        a0 = area(15360, C_DKS)
        k0 = area(16384, C_DKS)
        w1 = area(17408, C_DKS)
        att = area(11264, C_HEADS, 384)
        on = area(12800, NT, D)
        junkC = area(16896, N)
        fg = area(4096, D)

        def c_(name):
            return cst[:, CONST_AT[name][0]:CONST_AT[name][1]]

        ident = c_("ident")
        mask = c_("mask")
        mask_a1 = mask.rearrange("p (g c) -> p g c", c=CHUNK)[:, 0:5:2, :]
        mask_t0 = mask[:, 3 * CHUNK:5 * CHUNK]
        mask_b1 = mask[:, CHUNK:5 * CHUNK]
        tri = c_("tri").bitcast(U32)

        at = [0]

        def sm(*shape):
            n = int(np.prod(shape))
            a = small[:, at[0]:at[0] + n]
            at[0] += n
            assert at[0] <= 400
            return a.rearrange("p (a b) -> p a b", b=shape[1]) if len(shape) == 2 else a

        ssq = [sm(NT, 1), sm(NT, 4), sm(NT, 4)]
        ss, mean, root, tmp = (sm(NT) for _ in range(4))
        rstd = [sm(NT) for _ in range(3)]
        rq = sm(NT)
        mx_a, neg_a, sum_a, ex_a, r_a, es_a = (sm(NT, A_HEADS) for _ in range(6))
        mx_b, neg_b, sum_b, r_b = (sm(NT, B_MAPS) for _ in range(4))
        head = {k: [sm(4, NT) for _ in range(5)] for k in "BC"}
        lam_sum, lam_exp, lam = sm(2), sm(2), sm(1)

        acc = [[ctx.enter_context(nc.psum_tensor(f"acc{p}{t}", [P, N], F32)) for t in range(NT)] for p in range(2)]
        banks = [ctx.enter_context(nc.psum_tensor(f"task{i}", [P, N], F32)) for i in range(BANKS)]

        def bank(name):
            return banks[TASK[name] % BANKS]

        x_in = [sem(f"x_in{i}") for i in range(4)]
        consts_in, small_in, gate_in, fg_in = sem("consts_in"), sem("small_in"), sem("gate_in"), sem("fg_in")
        raw_in = [sem(f"raw_in{u}") for u in range(UNITS)]
        hi_done, lo_done = sem("hi_done"), sem("lo_done")
        half_used = sem("half_used")
        acc_free = sem("acc_free")
        task_ready = sem("task_ready")
        task_free = {"act": sem("task_free_act"), "dve": sem("task_free_dve")}
        xh_done = sem("xh_done")
        sq_done = sem("sq_done")
        head_sq = sem("head_sq")
        root_in, root_done = sem("root_in"), sem("root_done")
        sig_done = sem("sig_done")
        gain_ready = sem("gain_ready")
        lam_summed, lam_exped = sem("lam_summed"), sem("lam_exped")
        max_ready = sem("max_ready")
        exp_a_done, exp_b_done = sem("exp_a_done"), sem("exp_b_done")
        w_ready = sem("w_ready")
        pt_used = sem("pt_used")
        pv_free = sem("pv_free")
        lr_pad, lr_hi, lr_split = sem("lr_pad"), sem("lr_hi"), sem("lr_split")
        nz_ready, ln_done, gate_ready = sem("nz_ready"), sem("ln_done"), sem("gate_ready")
        scale_ready = sem("scale_ready")
        fin = [sem("fin0"), sem("fin1")]
        stored = sem("stored")
        act_step, dve_step = sem("act_step"), sem("dve_step")
        block = ctx.enter_context(nc.Block())

        def width_of(p):
            return BLOCKS[p - 1][4]

        def wait_free(eng, name):
            who, n = freed(TASK[name])
            eng.wait_ge(task_free[who], n)

        @block.sync
        def _(sp):
            xv = x.rearrange("o (t p) n -> (o p) t n", p=P)
            for i in range(4):
                sp.dma_start(xres[:, :, i * N:(i + 1) * N], xv[:, :, i * N:(i + 1) * N]).then_inc(x_in[i], 16)

            def load(matrix, first, width, p):
                rows = W[matrix].rearrange("o (u k p) n -> (o p) u k n", p=P, k=4)
                for u in range(UNITS):
                    if not isinstance(p, int):
                        sp.wait_ge(lo_done, (p - 2) * HALVES + (2 * u + 2))
                    cols = slice(first, first + width) if isinstance(first, int) else bass.ds(first, width)
                    sp.dma_start(raw[:, u, :, 0:width], rows[:, u, :, cols]).then_inc(raw_in[u], 16)

            load("ab_in", AK, 2 * A_KV * A_HD, 1)
            for kind, blocks in (("aq", 2), ("bq", 6), ("ag", 2), ("bg", 2), ("out0", 4), ("v", 4), ("q", 4), ("r", 4), ("out1", 4)):
                p0 = POS[kind, 0]
                _, _, matrix, col0, _ = BLOCKS[p0 - 1]
                with sp.Fori(0, blocks) as b:
                    load(matrix, b * N + col0, N, b + p0)
            ov = out.rearrange("o (t p) n -> (o p) t n", p=P)
            for t in range(NT):
                sp.wait_ge(fin[t], 1)
                sp.dma_start(ov[:, t, :], xres[:, t, :]).then_inc(stored, 16)
            sp.wait_ge(stored, 16 * NT)

        @block.gpsimd
        def _(pool):
            pool.dma_start(cst[:, :], consts).then_inc(consts_in, 16)
            for l in range(2):
                pool.dma_start(gain[:, 2 * l, :], gains[l]).then_inc(small_in, 16)
            pool.dma_start(hg[:, 0:2], bhg).then_inc(small_in, 16)
            pool.dma_start(hg[:, 2:6], chg).then_inc(small_in, 16)
            pool.dma_start(sink[:, :], sinks.broadcast_to([P, A_HEADS])).then_inc(small_in, 16)
            for i in range(4):
                pool.dma_start(lam_in[:, i, :], lams[i].broadcast_to([P, B_HD])).then_inc(small_in, 16)
            for pad in (lrh, lrl):
                nc.gpsimd.memset(pad[:, KT * C_RANK:].bitcast(F32), 0.0).then_inc(lr_pad, 1)
            pool.wait_ge(task_ready, TASK[f"y{KT - 1}"] + 1)
            pool.dma_start(g2[0:C_RANK, :], gate2).then_inc(gate_in, 16)
            pool.dma_start(gb, gate_b.broadcast_to([P, C_DKS])).then_inc(gate_in, 16)
            pool.dma_start(lrw.rearrange("p (k r) -> p k r", r=C_RANK),
                           w_c_in.rearrange("o (k p) n -> (o p) k n", p=P)[:, :, CLR:CLR + C_RANK]).then_inc(gate_in, 16)
            pool.wait_ge(task_ready, TASK[f"SC{C_HEADS - 1}"] + 1)
            pool.dma_start(fg, final_g.broadcast_to([P, D])).then_inc(fg_in, 16)

        @block.scalar
        def _(act):
            A = nc.scalar.activation
            steps = Steps(act, act_step)

            def halves(p, js, extra=None):
                w = width_of(p)
                for j in js:
                    n = (p - 1) * HALVES + j
                    if j % 2 == 0:
                        act.wait_ge(raw_in[j // 2], 16 * p)
                    if n >= SPLIT_RING:
                        act.wait_ge(half_used, n - SPLIT_RING + 1)
                    A(wh[:, j % SPLIT_RING, :, 0:w], raw[:, j // 2, 2 * (j % 2):2 * (j % 2) + 2, 0:w],
                      ACT.Copy).then_inc(hi_done, 1)
                    for _ in range(min(3, len(extra or ()))):
                        extra.pop(0)()

            def task(name):
                act.wait_ge(task_ready, TASK[name] + 1)
                return bank(name)

            def stationary(tag, g):
                for kt in range(KT):
                    A(xTh[:, kt, :], task(f"{tag}{kt}")[:, 0:S], ACT.Copy, scale=gain[:, g, kt:kt + 1]).then_inc(xh_done, 1)

            squares = {"row": 0, "head": 0}

            def square(kind, junk, src, total):
                s = sq_done if kind == "row" else head_sq
                if squares[kind]:
                    act.wait_ge(s, squares[kind])
                A(junk, src, ACT.Square, accum_out=total).then_inc(s, 1)
                squares[kind] += 1

            roots = [0]

            def sqrt(dst, src):
                roots[0] += 1
                act.wait_ge(root_in, roots[0])
                A(dst, src, ACT.Sqrt).then_inc(root_done, 1)

            def sigmoid(p, k):
                gates = [q for q, b in enumerate(BLOCKS[:p - 1], 1) if b[0] in ("ag", "bg", "r")]
                if gates:
                    act.wait_ge(acc_free, gates[-1] + 1)
                act.wait_ge(half_used, HALVES * p)
                for t in range(NT):
                    A(tA[:, t, :], acc[p % 2][t][:, :], ACT.Sigmoid, scale=rstd[k][:, t:t + 1]).then_inc(sig_done, 1)

            def copy_out(name, dst):
                A(dst, task(name)[:, :].rearrange("p (a b) -> p a b", b=dst.shape[2]), ACT.Copy).then_inc(task_free["act"], 1)

            jobs = []
            for t in range(NT):
                for h in range(A_HEADS):
                    def exp_a(h=h, t=t):
                        if (h, t) == (0, 0):
                            act.wait_ge(max_ready, 1)
                        cols = slice(0, P) if t == 0 else slice(P, 320)
                        A(pA[:, h, cols], pA[:, h, cols], ACT.Exp, bias=neg_a[:, t, h:h + 1], scale=A_HD ** -0.5,
                          accum_out=sum_a[:, t, h:h + 1]).then_inc(exp_a_done, 1)
                    jobs.append(exp_a)

            def exp_sinks():
                act.wait_ge(max_ready, 2)
                A(ex_a, es_a, ACT.Exp).then_inc(exp_a_done, 1)
            jobs.append(exp_sinks)
            for m in range(B_MAPS):
                for t in range(NT):
                    def exp_b(m=m, t=t):
                        if (m, t) == (0, 0):
                            act.wait_ge(max_ready, 3)
                        cols = slice(0, P) if t == 0 else slice(P, 384)
                        A(pB[:, m, cols], pB[:, m, cols], ACT.Exp, bias=neg_b[:, t, m:m + 1], scale=B_HD ** -0.5,
                          accum_out=sum_b[:, t, m:m + 1]).then_inc(exp_b_done, 1)
                    jobs.append(exp_b)

            def pt_out(name, n):
                b = task(name)
                if n >= 4:
                    act.wait_ge(pt_used, n - 3)
                if n < A_HEADS:
                    A(pT[:, n % 4, 0:S], b[:, 0:S], ACT.Copy)
                    A(pT[0:CHUNK, n % 4, S:384], b[0:CHUNK, S:384], ACT.Copy).then_inc(task_free["act"], 1)
                else:
                    A(pT[:, n % 4, :], b[:, 0:384], ACT.Copy).then_inc(task_free["act"], 1)

            def head_norm(k, h, names, junk, width):
                for t, (name, first) in enumerate(names):
                    square("head", junk, task(name)[:, first:first + width], head[k][0][:, h, t:t + 1])
                sqrt(head[k][2][:, h, :], head[k][1][:, h, :])

            def after_block(p):
                kind, c, _, _, _ = BLOCKS[p - 1]
                if kind == "kv":
                    sqrt(root, mean)
                elif kind in ("ag", "bg"):
                    sigmoid(p, 0)
                elif kind == "r":
                    sigmoid(p, 1)
                elif kind in ("out0", "out1"):
                    act.wait_ge(acc_free, p + 1)
                    for t in range(NT):
                        square("row", junkO, xres[:, t, c * N:(c + 1) * N], ssq[1 if kind == "out0" else 2][:, t, c:c + 1])

            def take_scores():
                copy_out("akT", akT)
                for name, dst in (("aqT", aqT), ("bqT", bqT), ("bkT", bkT)):
                    for g in range(4):
                        copy_out(f"{name}{g}", dst[:, 2 * g:2 * g + 2, :])

            def take_values():
                for h in range(1, A_HEADS, 2):
                    pt_out(f"PA{h}", h)
                for h in range(B_HEADS + 1):
                    if h < B_HEADS and h % 2:
                        pt_out(f"PB{h}", A_HEADS + h)
                    if h:
                        head_norm("B", h - 1, [(f"OB{h - 1}", 0), (f"OB{h - 1}", S)], junkB, S)

            def log_gates():
                for t in range(NT):
                    act.wait_ge(nz_ready, t + 1)
                    steps.did(A(gs[:, t, :], gs[:, t, :], ACT.Exp))
                for t in range(NT):
                    steps.wait(steps.n - NT + 1 + t)
                    A(gs[:, t, :], gs[:, t, :], ACT.Ln, bias=1.0).then_inc(ln_done, 1)

            def decays():
                s = 1.0 / GATE_TAU

                def exp(name, c, *dst, rows=P):
                    b = task(f"{name}{c}")
                    for i, (d, scale) in enumerate(dst):
                        ins = A(d[0:rows, c * N:(c + 1) * N], b[0:rows, :], ACT.Exp, scale=scale)
                    ins.then_inc(task_free["act"], 1)

                for name, dst, rows in (("cum0", ((qe[:, 0, :], s), (ke[:, 0, :], -s)), P), ("rev0", ((a0, s),), P),
                                        ("far0", ((k0, s),), CHUNK), ("cum1", ((qe[:, 1, :], s), (ke[:, 1, :], -s)), P),
                                        ("tail1", ((w1, s),), P)):
                    for c in range(2):
                        exp(name, c, *dst, rows=rows)

            def take_gla():
                for g in range(4):
                    copy_out(f"qeT{g}", qeT[:, 2 * g:2 * g + 2, :])
                for g in range(2):
                    b = task(f"a0T{g}")[:, :].rearrange("p (k c) -> p k c", c=P)
                    A(a0T[:, 4 * g:4 * g + 4, 0:CHUNK], b[:, :, 0:CHUNK], ACT.Copy)
                    A(kkT[:, 4 * g:4 * g + 4, CHUNK:P], b[:, :, CHUNK:P], ACT.Copy).then_inc(task_free["act"], 1)
                A(kkT[:, :, 0:CHUNK], task("k0T")[:, :].rearrange("p (k c) -> p k c", c=CHUNK), ACT.Copy).then_inc(task_free["act"], 1)
                for h in range(C_HEADS):
                    head_norm("C", h, [(f"OC{h}0", 0), (f"OC{h}1", 0)], junkC, C_DV)

            for p in range(1, NB + 1):
                kind, c, _, _, _ = BLOCKS[p - 1]
                soft = jobs if kind in ("bv", "ag") else None
                halves(p, range(4), soft if (kind, c) != ("bv", 0) else None)
                if p == 1:
                    for i in range(4):
                        act.wait_ge(x_in[i], 16)
                    for t in range(NT):
                        square("row", junk0, xres[:, t, :], ssq[0][:, t, 0:1])
                    act.wait_ge(lam_summed, 1)
                    A(lam_exp, lam_sum, ACT.Exp).then_inc(lam_exped, 1)
                    act.wait_ge(gain_ready, 1)
                    stationary("x", 0)
                else:
                    after_block(p - 1)
                if (kind, c) == ("bv", 0):
                    take_scores()
                if (kind, c) == ("bg", 0):
                    take_values()
                if (kind, c) == ("out0", 0):
                    stationary("y", 1)
                if (kind, c) == ("v", 0):
                    sqrt(root, mean)
                    stationary("h", 2)
                if (kind, c) == ("v", 1):
                    act.wait_ge(gate_in, 48)
                    A(lrh[:, 0:KT * C_RANK], lrw, ACT.Copy).then_inc(lr_hi, 1)
                if (kind, c) == ("v", 2):
                    log_gates()
                if (kind, c) == ("q", 0):
                    decays()
                if (kind, c) == ("r", 0):
                    take_gla()
                if (kind, c) == ("out1", 0):
                    stationary("u", 3)
                halves(p, range(4, 8), soft)
            after_block(NB)
            sqrt(root, mean)
            act.wait_ge(scale_ready, 1)
            A(xres[:, 1, :], xres[:, 1, :], ACT.Copy, scale=rstd[2][:, 1:2]).then_inc(fin[1], 1)

        @block.vector
        def _(dve):
            V = nc.vector
            steps = Steps(dve, dve_step)

            def halves(p, js, extra=None):
                w = width_of(p)
                for j in js:
                    dve.wait_ge(hi_done, (p - 1) * HALVES + j + 1)
                    V.tensor_tensor(wl[:, j % SPLIT_RING, :, 0:w], raw[:, j // 2, 2 * (j % 2):2 * (j % 2) + 2, 0:w],
                                    wh[:, j % SPLIT_RING, :, 0:w].bitcast(F32), ALU.subtract).then_inc(lo_done, 1)
                    if extra:
                        extra.pop(0)()

            def task(name):
                dve.wait_ge(task_ready, TASK[name] + 1)
                return bank(name)

            def emptied(ins):
                ins.then_inc(task_free["dve"], 1)

            highs = [0]

            def stationary(tag, g):
                for kt in range(KT):
                    b = task(f"{tag}{kt}")
                    highs[0] += 1
                    dve.wait_ge(xh_done, highs[0])
                    emptied(V.scalar_tensor_tensor(out=xTl[:, kt, :], in0=b[:, 0:S], scalar=gain[:, g, kt:kt + 1],
                                                   in1=xTh[:, kt, :].bitcast(F32), op0=ALU.mult, op1=ALU.subtract))

            def then(ins):
                steps.did(ins)
                steps.wait()

            roots = [0]

            def rsqrt(dst, total, mean_, root_, tmp_, inv_n, eps):
                V.tensor_scalar(mean_, total, inv_n, eps, ALU.mult, ALU.add).then_inc(root_in, 1)
                roots[0] += 1
                dve.wait_ge(root_done, roots[0])
                then(V.reciprocal(dst, root_))
                then(V.tensor_tensor(tmp_, dst, dst, ALU.mult))
                then(V.tensor_tensor(tmp_, tmp_, mean_, ALU.mult))
                then(V.tensor_scalar(tmp_, tmp_, -0.5, 1.5, ALU.mult, ALU.add))
                then(V.tensor_tensor(dst, dst, tmp_, ALU.mult))

            def row_norm(k):
                total = ssq[k][:, :, 0]
                if k:
                    then(V.reduce_sum(ss, ssq[k], AX_X))
                    total = ss
                rsqrt(rstd[k], total, mean, root, tmp, 1.0 / D, NORM_EPS)

            def head_norm(k, h, width):
                sq, mean_, root_, tmp_, r = (a[:, h, :] for a in head[k])
                rsqrt(r, sq, mean_, root_, tmp_, 1.0 / width, HEAD_EPS)

            def rotate(src, dst, cos, sin):
                n, half = src.shape[1], src.shape[3]
                size = n * 2 * half
                b4 = tB[:, 0:size].rearrange("p (n a c) -> p n a c", a=2, c=half)
                c4 = tC[:, 0:size].rearrange("p (n a c) -> p n a c", a=2, c=half)
                cos_all = cos.unsqueeze(1).broadcast_to([P, 2 * n, half])
                sin_all = sin.unsqueeze(1).broadcast_to([P, n, half])
                steps.did(V.tensor_tensor(b4.rearrange("p n a c -> p (n a) c"), src.rearrange("p n a c -> p (n a) c"), cos_all, ALU.mult))
                steps.did(V.scalar_tensor_tensor(out=c4[:, :, 0, :], in0=src[:, :, 1, :], scalar=-1.0, in1=sin_all,
                                                 op0=ALU.mult, op1=ALU.mult))
                then(V.tensor_tensor(c4[:, :, 1, :], src[:, :, 0, :], sin_all, ALU.mult))
                return V.tensor_tensor(dst, b4, c4, ALU.add)

            def table(name, t):
                half, first = (32, 0) if name == "A" else (64, 128)
                cos = rope[:, first + t * half:first + (t + 1) * half]
                sin = rope[:, first + NT * half + t * half:first + NT * half + (t + 1) * half]
                return cos, sin

            def after_block(p):
                kind, c, _, _, _ = BLOCKS[p - 1]
                cols = slice(c * N, (c + 1) * N)
                dve.wait_ge(half_used, HALVES * p)
                o = acc[p % 2]
                if kind == "kv":
                    dve.wait_ge(sq_done, NT)
                    row_norm(0)
                    dve.wait_ge(consts_in, 16)
                    for t in range(NT):
                        for dst, src in zip(table("A", t) + table("B", t), ("cosA", "sinA", "cosB", "sinB")):
                            half = dst.shape[1]
                            steps.did(V.tensor_scalar(dst, c_(src)[:, t * half:(t + 1) * half], rstd[0][:, t:t + 1], None, ALU.mult))
                    steps.wait()
                    for t in range(NT):
                        cos, sin = table("A", t)
                        then(rotate(o[t][:, 0:P].rearrange("p (n a c) -> p n a c", n=A_KV, a=2),
                                    akr[:, t, :, 0, :].rearrange("p n (a c) -> p n a c", a=2), cos, sin))
                        steps.did(V.tensor_copy(akr[:, t, :, 1, :], akr[:, t, :, 0, :]))
                    for rows, src, kt in ((slice(0, P), (0, slice(0, P)), 0), (slice(0, CHUNK), (0, slice(CHUNK, P)), 1),
                                          (slice(CHUNK, P), (1, slice(0, CHUNK)), 1), (slice(0, CHUNK), (1, slice(CHUNK, P)), 2)):
                        ins = V.tensor_scalar(av[rows, kt, :], o[src[0]][src[1], P:2 * P], rstd[0][src[1], src[0]:src[0] + 1], None, ALU.mult)
                        if kt != 2:
                            steps.did(ins)
                elif kind in ("aq", "bq", "bk"):
                    name, dst = ("A", aq) if kind == "aq" else ("B", bq if kind == "bq" else bk)
                    for t in range(NT):
                        cos, sin = table(name, t)
                        shape = dict(a=2, c=cos.shape[1])
                        ins = rotate(o[t][:, :].rearrange("p (n a c) -> p n a c", **shape),
                                     dst[:, t, cols].rearrange("p (n a c) -> p n a c", **shape), cos, sin)
                        if t == 0:
                            then(ins)
                elif kind == "bv":
                    for t in range(NT):
                        ins = V.tensor_scalar(bv[:, t, cols], o[t][:, :], rstd[0][:, t:t + 1], None, ALU.mult)
                elif kind in ("ag", "bg", "r"):
                    n = sum(b[0] in ("ag", "bg", "r") for b in BLOCKS[:p])
                    r = rstd[1 if kind == "r" else 0]
                    for t in range(NT):
                        dve.wait_ge(sig_done, NT * (n - 1) + t + 1)
                        if kind == "ag":
                            ins = V.scalar_tensor_tensor(out=ya[:, t, cols], in0=o[t][:, :], scalar=r[:, t:t + 1],
                                                         in1=tA[:, t, :], op0=ALU.mult, op1=ALU.mult)
                        else:
                            y = (yb if kind == "bg" else on)[:, t, cols]
                            then(V.scalar_tensor_tensor(out=tB[:, :], in0=o[t][:, :], scalar=r[:, t:t + 1],
                                                        in1=tA[:, t, :], op0=ALU.mult, op1=ALU.mult))
                            ins = V.tensor_tensor(y, y, tB[:, :], ALU.mult)
                            if t == 0:
                                then(ins)
                elif kind in ("out0", "out1"):
                    for t in range(NT):
                        ins = V.tensor_tensor(xres[:, t, cols], o[t][:, :], xres[:, t, cols], ALU.add)
                elif kind == "v":
                    for t in range(NT):
                        ins = V.tensor_scalar(v[:, t, cols], o[t][:, :], rstd[1][:, t:t + 1], None, ALU.mult)
                elif kind == "q":
                    if c == 0:
                        wait_free(dve, "tail11")
                    for t in range(NT):
                        steps.did(V.scalar_tensor_tensor(out=qe[:, t, cols], in0=o[t][:, :], scalar=rq[:, t:t + 1],
                                                         in1=qe[:, t, cols], op0=ALU.mult, op1=ALU.mult))
                    late = slice(CHUNK, P)
                    ins = V.scalar_tensor_tensor(out=w1[late, cols], in0=o[1][late, :], scalar=rq[late, 1:2],
                                                 in1=w1[late, cols], op0=ALU.mult, op1=ALU.mult)
                elif kind == "k":
                    early = slice(0, CHUNK)
                    for t in range(NT):
                        steps.did(V.scalar_tensor_tensor(out=ke[:, t, cols], in0=o[t][:, :], scalar=rstd[1][:, t:t + 1],
                                                         in1=ke[:, t, cols], op0=ALU.mult, op1=ALU.mult))
                    steps.did(V.scalar_tensor_tensor(out=a0[:, cols], in0=o[0][:, :], scalar=rstd[1][:, 0:1],
                                                     in1=a0[:, cols], op0=ALU.mult, op1=ALU.mult))
                    steps.did(V.scalar_tensor_tensor(out=k0[early, cols], in0=o[0][early, :], scalar=rstd[1][early, 0:1],
                                                     in1=k0[early, cols], op0=ALU.mult, op1=ALU.mult))
                    ins = V.scalar_tensor_tensor(out=w1[early, cols], in0=o[1][early, :], scalar=rstd[1][early, 1:2],
                                                 in1=w1[early, cols], op0=ALU.mult, op1=ALU.mult)
                ins.then_inc(acc_free, 1)

            def masked(name, out_, src, mask_, total):
                return V.tensor_tensor_reduce(out=out_, in0=src, in1=mask_, scale=1.0, scalar=-3.0e38, op0=ALU.add,
                                              op1=ALU.max, accum_out=total)

            def take_scores():
                g3 = dict(c=CHUNK)
                for h in range(A_HEADS):
                    b = task(f"SA{h}")
                    steps.did(masked("A", pA[:, h, 0:P], b[:, 0:P], mask_t0, mx_a[:, 0, h:h + 1]))
                    emptied(masked("A", pA[:, h, P:320].rearrange("p (g c) -> p g c", **g3),
                                   b[:, P:320].rearrange("p (g c) -> p g c", **g3), mask_a1, mx_a[:, 1, h:h + 1]))
                for m in range(B_MAPS):
                    b = task(f"SB{m}")
                    steps.did(masked("B", pB[:, m, 0:P], b[:, 0:P], mask_t0, mx_b[:, 0, m:m + 1]))
                    emptied(masked("B", pB[:, m, P:384], b[:, P:384], mask_b1, mx_b[:, 1, m:m + 1]))
                steps.wait()
                wait_free(dve, f"SB{B_MAPS - 1}")
                then(V.scalar_tensor_tensor(out=es_a, in0=mx_a, scalar=A_HD ** -0.5,
                                            in1=sink[:, :].unsqueeze(1).broadcast_to([P, NT, A_HEADS]), op0=ALU.mult, op1=ALU.max))
                V.tensor_scalar(neg_a, es_a, -1.0, None, ALU.mult).then_inc(max_ready, 1)
                dve.wait_ge(max_ready, 1)
                V.tensor_tensor(es_a, sink[:, :].unsqueeze(1).broadcast_to([P, NT, A_HEADS]), neg_a, ALU.add).then_inc(max_ready, 1)
                V.tensor_scalar(neg_b, mx_b, -(B_HD ** -0.5), None, ALU.mult).then_inc(max_ready, 1)

            jobs = []
            for h in range(B_HEADS):
                for t in range(NT):
                    def differ(h=h, t=t):
                        if (h, t) == (0, 0):
                            dve.wait_ge(exp_b_done, NT * B_MAPS)
                            then(V.reciprocal(r_b, sum_b))
                            odd = r_b[:, :, 1:B_MAPS:2]
                            then(V.tensor_scalar(odd, odd, lam, None, ALU.mult))
                        cols = slice(0, P) if t == 0 else slice(P, 384)
                        w = cols.stop - cols.start
                        then(V.tensor_scalar(tC[:, 0:w], pB[:, 2 * h + 1, cols], r_b[:, t, 2 * h + 1:2 * h + 2], None, ALU.mult))
                        V.scalar_tensor_tensor(out=pB[:, 2 * h, cols], in0=pB[:, 2 * h, cols], scalar=r_b[:, t, 2 * h:2 * h + 1],
                                               in1=tC[:, 0:w], op0=ALU.mult, op1=ALU.subtract).then_inc(w_ready, 1)
                        dve.wait_ge(w_ready, NT * h + t + 1)
                    jobs.append(differ)

            def pt_out(name, n):
                b = task(name)
                if n >= 4:
                    dve.wait_ge(pt_used, n - 3)
                if n < A_HEADS:
                    V.tensor_copy(pT[:, n % 4, 0:S], b[:, 0:S])
                    emptied(V.tensor_copy(pT[0:CHUNK, n % 4, S:384], b[0:CHUNK, S:384]))
                else:
                    emptied(V.tensor_copy(pT[:, n % 4, :], b[:, 0:384]))

            def take_values():
                for h in range(0, A_HEADS, 2):
                    pt_out(f"PA{h}", h)
                dve.wait_ge(exp_a_done, NT * A_HEADS + 1)
                then(V.tensor_tensor(r_a, sum_a, ex_a, ALU.add))
                then(V.reciprocal(r_a, r_a))
                for g in range(A_KV):
                    dve.wait_ge(pt_used, A_GROUP * (g + 1))
                    for t in range(NT):
                        then(V.tensor_tensor(tB[:, :].rearrange("p (h d) -> p h d", d=A_HD),
                                             acc[g][t][:, :].rearrange("p (h d) -> p h d", d=A_HD),
                                             r_a[:, t, g * A_GROUP:(g + 1) * A_GROUP].unsqueeze(2).broadcast_to([P, A_GROUP, A_HD]),
                                             ALU.mult))
                        y = ya[:, t, g * N:(g + 1) * N]
                        V.tensor_tensor(y, y, tB[:, :], ALU.mult).then_inc(pv_free, 1)
                        dve.wait_ge(pv_free, NT * g + t + 1)
                for h in range(B_HEADS + 1):
                    if h < B_HEADS and h % 2 == 0:
                        pt_out(f"PB{h}", A_HEADS + h)
                    if h:
                        b = task(f"OB{h - 1}")
                        dve.wait_ge(head_sq, NT * h)
                        head_norm("B", h - 1, 2 * B_HD)
                        for t in range(NT):
                            ins = V.tensor_scalar(yb[:, t, (h - 1) * S:h * S], b[:, t * S:(t + 1) * S],
                                                  head["B"][4][:, h - 1, t:t + 1], None, ALU.mult)
                            if t == 0:
                                steps.did(ins)
                        emptied(ins)

            def take_gate_inputs():
                emptied(V.tensor_copy(lrT[0:C_RANK, :], task("lr")[0:C_RANK, 0:S]))
                dve.wait_ge(gate_in, 48)
                for t in range(NT):
                    for c in range(2):
                        cols = slice(c * N, (c + 1) * N)
                        emptied(V.scalar_tensor_tensor(out=zs[:, t, cols], in0=task(f"z{t}{c}")[:, :], scalar=rstd[1][:, t:t + 1],
                                                       in1=gb[:, cols], op0=ALU.mult, op1=ALU.add))
                    wait_free(dve, f"z{t}1")
                    V.scalar_tensor_tensor(out=gs[:, t, :], in0=zs[:, t, :], scalar=-1.0, in1=zs[:, t, :],
                                           op0=ALU.mult, op1=ALU.min).then_inc(nz_ready, 1)

            def log_sigmoid():
                for t in range(NT):
                    dve.wait_ge(ln_done, t + 1)
                    V.scalar_tensor_tensor(out=gs[:, t, :], in0=zs[:, t, :], scalar=0.0, in1=gs[:, t, :],
                                           op0=ALU.min, op1=ALU.subtract).then_inc(gate_ready, 1)

            def take_gla():
                for g in range(4):
                    emptied(V.tensor_copy(keT[:, 2 * g:2 * g + 2, :], task(f"keT{g}")[:, :].rearrange("p (k c) -> p k c", c=S)))
                for g in range(2):
                    emptied(V.tensor_copy(w1T[:, 4 * g:4 * g + 4, :], task(f"w1T{g}")[:, :].rearrange("p (k c) -> p k c", c=P)))
                b = task("SC0")
                then(V.memset(att, 0.0))
                for h in range(C_HEADS):
                    b = task(f"SC{h}")
                    for t in range(NT):
                        steps.did(V.copy_predicated(att[:, h, t * P:(t + 1) * P], tri, b[:, t * P:(t + 1) * P]))
                    emptied(V.tensor_copy(att[:, h, S:384], b[:, S:384]))
                for h in range(C_HEADS):
                    dve.wait_ge(head_sq, NT * (B_HEADS + h + 1))
                    head_norm("C", h, C_DV)
                    for t in range(NT):
                        emptied(V.tensor_scalar(on[:, t, h * N:(h + 1) * N], task(f"OC{h}{t}")[:, :],
                                                head["C"][4][:, h, t:t + 1], None, ALU.mult))

            def final_gain(c):
                dve.wait_ge(fg_in, 16)
                dve.wait_ge(sq_done, NT * (1 + 4 + c + 1))
                cols = slice(c * N, (c + 1) * N)
                return V.tensor_tensor(xres[:, :, cols], xres[:, :, cols],
                                       fg[:, cols].unsqueeze(1).broadcast_to([P, NT, N]), ALU.mult)

            V.memset(small[:, 399:400], 0.0).then_inc(acc_free, 1)
            dve.wait_ge(small_in, 9 * 16)
            steps.did(V.memset(gain[:, 1, 0:8], 1.0))
            steps.did(V.tensor_scalar(gain[:, 1, 8:16].rearrange("p (h k) -> p h k", k=2),
                                      hg[:, 0:2].unsqueeze(1).broadcast_to([P, B_HEADS, 2]), 1.0 - LAMBDA_INIT, None, ALU.mult))
            V.tensor_copy(gain[:, 3, :].rearrange("p (h k) -> p h k", k=4),
                          hg[:, 2:6].unsqueeze(1).broadcast_to([P, C_HEADS, 4])).then_inc(gain_ready, 1)
            for i in range(2):
                ins = V.tensor_tensor_reduce(out=tB[:, i * B_HD:(i + 1) * B_HD], in0=lam_in[:, 2 * i, :], in1=lam_in[:, 2 * i + 1, :],
                                             scale=1.0, scalar=0.0, op0=ALU.mult, op1=ALU.add, accum_out=lam_sum[:, i:i + 1])
                if i == 0:
                    then(ins)
            ins.then_inc(lam_summed, 1)
            dve.wait_ge(lam_exped, 1)
            then(V.tensor_tensor(lam, lam_exp[:, 0:1], lam_exp[:, 1:2], ALU.subtract))
            then(V.tensor_scalar(lam, lam, LAMBDA_INIT, None, ALU.add))

            for p in range(1, NB + 1):
                kind, c, _, _, _ = BLOCKS[p - 1]
                extra = jobs if (kind, c) == ("ag", 1) else None
                halves(p, range(4), extra)
                if p == 1:
                    stationary("x", 0)
                else:
                    after_block(p - 1)
                if (kind, c) == ("bv", 0):
                    take_scores()
                if (kind, c) == ("bg", 0):
                    while jobs:
                        jobs.pop(0)()
                    take_values()
                if (kind, c) == ("out0", 0):
                    stationary("y", 1)
                if (kind, c) == ("v", 0):
                    dve.wait_ge(sq_done, NT * (1 + 4))
                    row_norm(1)
                    then(V.tensor_scalar(rq, rstd[1], C_DK ** -0.5, None, ALU.mult))
                    stationary("h", 2)
                if (kind, c) == ("v", 1):
                    dve.wait_ge(lr_hi, 1)
                    V.tensor_tensor(lrl[:, 0:KT * C_RANK], lrw, lrh[:, 0:KT * C_RANK].bitcast(F32), ALU.subtract).then_inc(lr_split, 1)
                if (kind, c) == ("v", 2):
                    take_gate_inputs()
                if (kind, c) == ("r", 0):
                    take_gla()
                if (kind, c) == ("out1", 0):
                    stationary("u", 3)
                if kind == "out1" and c >= 2:
                    steps.did(final_gain(c - 2))
                halves(p, range(4, 8), extra)
                if (kind, c) == ("v", 2):
                    log_sigmoid()
            after_block(NB)
            steps.did(final_gain(2))
            dve.wait_ge(sq_done, NT * (1 + 4 + 4))
            row_norm(2)
            final_gain(3).then_inc(scale_ready, 1)
            dve.wait_ge(scale_ready, 1)
            V.tensor_scalar(xres[:, 0, :], xres[:, 0, :], rstd[2][:, 0:1], None, ALU.mult).then_inc(fin[0], 1)

        @block.tensor
        def _(pe):
            MM = nc.tensor.matmul

            def half(p, j, par, w, tag):
                pe.wait_ge(lo_done, p * HALVES + (j + 1 - HALVES))
                wait_free(pe, f"{tag}{2 * j + 1}")
                for kt in (2 * j, 2 * j + 1):
                    high, low = (a[:, j % SPLIT_RING, kt % 2, 0:w] for a in (wh, wl))
                    for t in range(NT):
                        o = acc[par][t][:, 0:w]
                        tokens = slice(t * P, (t + 1) * P)
                        MM(o, xTh[:, kt, tokens], high, start=kt == 0, stop=False)
                        MM(o, xTh[:, kt, tokens], low, start=False, stop=False)
                        ins = MM(o, xTl[:, kt, tokens], high, start=False, stop=kt == KT - 1)
                ins.then_inc(half_used, 1)

            def two_blocks(p, par, tag):
                for i in range(2):
                    pe.wait_ge(acc_free, p + (i - 1))
                    for j in range(HALVES):
                        half(p + i, j, (par + i) % 2, N, tag)

            def pairs(kind, n, tag):
                p0 = POS[kind, 0]
                if n == 1:
                    two_blocks(p0, p0 % 2, tag)
                    return
                with pe.Fori(0, n) as i:
                    two_blocks(i * 2 + p0, p0 % 2, tag)

            def begin(name):
                k = TASK[name]
                if k >= BANKS:
                    wait_free(pe, TASKS[k - BANKS][0])
                return bank(name)

            def done(ins):
                ins.then_inc(task_ready, 1)

            def turn(name, sources, rows=P):
                b = begin(name)
                for i, s in enumerate(sources):
                    ins = nc.tensor.transpose(b[:, i * rows:(i + 1) * rows], s, ident[0:rows, 0:rows])
                done(ins)

            def first_pair(p, w, tag, tile, blocks):
                def turns(kts):
                    for kt in kts:
                        turn(f"{tag}{kt}", [tile(kt, t) for t in range(NT)])

                turns(range(4))
                for i in range(blocks):
                    if p + i > 2:
                        pe.wait_ge(acc_free, p + i - 1)
                    for j in range(HALVES):
                        half(p + i, j, (p + i) % 2, w, tag)
                        if i == 0 and j < 3:
                            turns(range(4 * j + 4, 4 * j + 8))

            pe.wait_ge(consts_in, 16)
            for i in range(4):
                pe.wait_ge(x_in[i], 16)
            first_pair(1, width_of(1), "x", lambda kt, t: xres[:, t, kt * P:(kt + 1) * P], 1)
            pairs("aq", 3, "x")

            pe.wait_ge(acc_free, POS["bk", 1] + 1)
            turn("akT", [akr[:, t, g, :, :].rearrange("p a d -> p (a d)") for g in range(A_KV) for t in range(NT)])

            def turn_heads(name, g, src):
                turn(f"{name}{g}", [src[:, t, h * P:(h + 1) * P] for h in (2 * g, 2 * g + 1) for t in range(NT)])

            def scores_a(h):
                b = begin(f"SA{h}")
                wait_free(pe, f"aqT{h // 4}")
                rows = slice(A_HD * (h % 2), A_HD * (h % 2) + A_HD)
                MM(b[:, 0:P], aqT[rows, h // 2, 0:P], akT[rows, h // A_GROUP, 0:P], start=True, stop=True)
                done(MM(b[:, P:320], aqT[rows, h // 2, P:S], akT[rows, h // A_GROUP, CHUNK:S], start=True, stop=True))

            for g in range(4):
                turn_heads("aqT", g, aq)
                if g:
                    for h in range(4 * g - 4, 4 * g):
                        scores_a(h)
            for g in range(4):
                turn_heads("bqT", g, bq)
                if g == 0:
                    for h in range(12, 16):
                        scores_a(h)
            for g in range(4):
                turn_heads("bkT", g, bk)
            for m in range(B_MAPS):
                b = begin(f"SB{m}")
                wait_free(pe, f"bkT{m // 2}")
                MM(b[:, 0:P], bqT[:, m, 0:P], bkT[:, m, 0:P], start=True, stop=True)
                done(MM(b[:, P:384], bqT[:, m, P:S], bkT[:, m, :], start=True, stop=True))

            pairs("bv", 2, "x")

            pe.wait_ge(acc_free, POS["ag", 1] + 1)
            pe.wait_ge(exp_a_done, NT * A_HEADS)

            def values_a(h):
                wait_free(pe, f"PA{h}")
                g, slot = h // A_GROUP, pT[:, h % 4, :]
                cols = slice((h % A_GROUP) * A_HD, (h % A_GROUP + 1) * A_HD)
                vals = av[:, :, g * A_HD:(g + 1) * A_HD]
                MM(acc[g][0][:, cols], slot[:, 0:P], vals[:, 0, :], start=True, stop=True)
                MM(acc[g][1][:, cols], slot[:, P:S], vals[:, 1, :], start=True, stop=False)
                MM(acc[g][1][:, cols], slot[0:CHUNK, S:384], vals[0:CHUNK, 2, :], start=False, stop=True).then_inc(pt_used, 1)

            for h in range(A_HEADS + 1):
                if h < A_HEADS:
                    b = begin(f"PA{h}")
                    nc.tensor.transpose(b[:, 0:P], pA[:, h, 0:P], ident)
                    nc.tensor.transpose(b[:, P:S], pA[:, h, P:S], ident)
                    done(nc.tensor.transpose(b[0:CHUNK, S:384], pA[:, h, S:320], ident))
                if h:
                    values_a(h - 1)

            def values_b(h):
                b = begin(f"OB{h}")
                wait_free(pe, f"PB{h}")
                slot, cols = pT[:, (A_HEADS + h) % 4, :], slice(h * S, (h + 1) * S)
                MM(b[:, 0:S], slot[:, 0:P], bv[:, 0, cols], start=True, stop=True)
                MM(b[:, S:2 * S], slot[:, P:S], bv[:, 0, cols], start=True, stop=False)
                ins = MM(b[:, S:2 * S], slot[:, S:384], bv[:, 1, cols], start=False, stop=True)
                done(ins)

            for h in range(B_HEADS + 1):
                if h < B_HEADS:
                    pe.wait_ge(w_ready, NT * (h + 1))
                    turn(f"PB{h}", [pB[:, 2 * h, i * P:(i + 1) * P] for i in range(3)])
                if h:
                    values_b(h - 1)
            pe.wait_ge(pv_free, NT * A_KV)
            pairs("bg", 1, "x")

            pe.wait_ge(acc_free, POS["bg", 1] + 1)
            p = POS["out0", 0]
            first_pair(p, N, "y", lambda kt, t: (ya if kt < 8 else yb)[:, t, kt % 8 * P:(kt % 8 + 1) * P], 2)
            pairs2 = POS["out0", 2]
            two_blocks(pairs2, pairs2 % 2, "y")

            pe.wait_ge(acc_free, POS["out0", 3] + 1)
            first_pair(POS["v", 0], N, "h", lambda kt, t: xres[:, t, kt * P:(kt + 1) * P], 2)
            pe.wait_ge(lr_split, 1)
            pe.wait_ge(lr_pad, 2)
            b = begin("lr")
            for kt in range(KT):
                cols = slice(C_RANK * kt, C_RANK * kt + 80)
                for i, (wgt, a) in enumerate(((lrh, xTh), (lrh, xTl), (lrl, xTh))):
                    ins = MM(b[0:80, 0:S], wgt[:, cols], a[:, kt, :], start=kt + i == 0, stop=kt == KT - 1 and i == 2)
            done(ins)
            wait_free(pe, "lr")
            pe.wait_ge(gate_in, 48)
            for t in range(NT):
                for c in range(2):
                    done(MM(begin(f"z{t}{c}")[:, :], lrT[0:C_RANK, t * P:(t + 1) * P], g2[0:C_RANK, c * N:(c + 1) * N],
                            start=True, stop=True))
            two_blocks(POS["v", 2], POS["v", 2] % 2, "h")
            pe.wait_ge(gate_ready, NT)
            for name, t, mat, rows in (("cum0", 0, "cum64", P), ("rev0", 0, "rev64", P), ("far0", 0, "rev128", CHUNK),
                                       ("cum1", 1, "cum64", P), ("tail1", 1, "tail", P)):
                for c in range(2):
                    done(MM(begin(f"{name}{c}")[0:rows, :], c_(mat), gs[:, t, c * N:(c + 1) * N], start=True, stop=True))
            pairs("q", 2, "h")

            pe.wait_ge(acc_free, POS["k", 1] + 1)
            for name, src in (("qeT", qe), ("keT", ke)):
                for g in range(4):
                    turn_heads(name, g, src)
            for name, src in (("a0T", a0), ("w1T", w1)):
                for g in range(2):
                    turn(f"{name}{g}", [src[:, k * P:(k + 1) * P] for k in range(4 * g, 4 * g + 4)])
            turn("k0T", [k0[0:CHUNK, k * P:(k + 1) * P] for k in range(8)], rows=CHUNK)
            wait_free(pe, "w1T1")
            wait_free(pe, "k0T")
            for h in range(C_HEADS):
                b = begin(f"SC{h}")
                ks = (2 * h, 2 * h + 1)
                for t in range(NT):
                    first = t * P
                    for i, k in enumerate(ks):
                        MM(b[:, first:first + P], keT[:, k, first:first + P], qeT[:, k, first:first + P], start=i == 0, stop=i == 1)
                    decayed = a0T if t == 0 else w1T
                    for i, k in enumerate(ks):
                        MM(b[0:CHUNK, first + CHUNK:first + P], decayed[:, k, 0:CHUNK], qeT[:, k, first + CHUNK:first + P],
                           start=i == 0, stop=i == 1)
                for i, k in enumerate(ks):
                    MM(b[:, S:S + CHUNK], kkT[:, k, :], qeT[:, k, P:P + CHUNK], start=i == 0, stop=i == 1)
                for i, k in enumerate(ks):
                    ins = MM(b[:, S + CHUNK:384], kkT[:, k, :], w1T[:, k, CHUNK:P], start=i == 0, stop=i == 1)
                done(ins)
            for h in range(C_HEADS):
                cols = slice(h * C_DV, (h + 1) * C_DV)
                b = begin(f"OC{h}0")
                wait_free(pe, f"SC{h}")
                done(MM(b[:, :], att[:, h, 0:P], v[:, 0, cols], start=True, stop=True))
                b = begin(f"OC{h}1")
                MM(b[:, :], att[:, h, S:384], v[:, 0, cols], start=True, stop=False)
                done(MM(b[:, :], att[:, h, P:S], v[:, 1, cols], start=False, stop=True))
            pairs("r", 2, "h")
            pe.wait_ge(acc_free, POS["r", 3] + 1)
            first_pair(POS["out1", 0], N, "u", lambda kt, t: on[:, t, kt * P:(kt + 1) * P], 2)
            two_blocks(POS["out1", 2], POS["out1", 2] % 2, "u")


def kernel(**inputs):
    import concourse.bacc as bacc
    from concourse.bass_utils import run_bass_kernel_spmd

    a = {k: np.ascontiguousarray(i) for k, i in inputs.items()}
    arrays = {
        "x": a["x"],
        "consts": constants(),
        "norm_g": np.ascontiguousarray(a["norm_g"].reshape(2, KT, P).transpose(0, 2, 1)),
        "b_head_g": np.ascontiguousarray(a["b_head_g"].reshape(2, P).T),
        "c_head_g": np.ascontiguousarray(a["c_head_g"].reshape(4, P).T),
        "final_g": a["final_g"].reshape(1, D),
        "ab_w_in": a["ab_w_in"], "ab_w_out": a["ab_w_out"], "c_w_in": a["c_w_in"], "c_w_out": a["c_w_out"],
        "a_sinks": a["a_sinks"], "lq1": a["b_lq1"], "lk1": a["b_lk1"], "lq2": a["b_lq2"], "lk2": a["b_lk2"],
        "gate2": a["c_w_gate2"].reshape(C_RANK, C_DKS), "gate_b": a["c_gate_b"].reshape(1, C_DKS),
    }
    nc = bacc.Bacc("TRN2", target_bir_lowering=False, num_devices=1)
    d = {k: nc.dram_tensor(f"in_{k}", i.shape, mybir.dt.from_np(i.dtype), kind="ExternalInput").ap() for k, i in arrays.items()}
    out = nc.dram_tensor("out", (1, S, D), F32, kind="ExternalOutput").ap()
    build(nc, d["x"], d["consts"], [d["norm_g"][i] for i in range(2)], d["b_head_g"], d["c_head_g"], d["final_g"],
          d["ab_w_in"], d["ab_w_out"], d["c_w_in"], d["c_w_out"], d["a_sinks"],
          [d[k] for k in ("lq1", "lk1", "lq2", "lk2")], d["gate2"], d["gate_b"], out)
    r = run_bass_kernel_spmd(nc, [{f"in_{k}": i for k, i in arrays.items()}], core_ids=[0])
    return r.results[0]["out"]
```

```python
import math
from contextlib import ExitStack

import numpy as np

import concourse.bass as bass
from concourse import mybir

F32 = mybir.dt.float32
F32R = mybir.dt.float32r
U32 = mybir.dt.uint32
ALU = mybir.AluOpType
ACT = mybir.ActivationFunctionType
AX_X = mybir.AxisListType.X

P = 128
D = 2048
S = 256
NT = S // P
KT = D // P
CHUNK = 64
A_HD, A_HEADS, A_KV = 64, 16, 2
A_GROUP = A_HEADS // A_KV
B_HD, B_HEADS = 128, 4
B_MAPS = 2 * B_HEADS
C_HEADS, C_DK, C_DV, C_RANK = 4, 256, 512, 16
C_DKS = C_HEADS * C_DK
GATE_TAU = 16.0
THETA = 10000.0
NEG = -1e30
NORM_EPS, HEAD_EPS = 1e-6, 1e-5
LAMBDA_INIT = 0.8 - 0.6 * math.exp(-0.3 * 0)

N = 512
HALVES = 8
UNITS = 4
SPLIT_RING = 4

AQ, AK = 0, A_HEADS * A_HD
AG = AK + 2 * A_KV * A_HD
BQ = AG + D // 2
BK, BV, BG = BQ + 1024, BQ + 2048, BQ + 3072
CQ, CK, CV, CR = 0, C_DKS, 2 * C_DKS, 2 * C_DKS + C_HEADS * C_DV
CLR = CR + C_HEADS * C_DV

BLOCKS = [("kv", 0, "ab_in", AK, 2 * A_KV * A_HD)]
BLOCKS += [(k, c, "ab_in", at + N * c, N) for k, at in (("aq", AQ), ("bq", BQ), ("bk", BK), ("ag", AG), ("bv", BV), ("bg", BG)) for c in range(2)]
BLOCKS += [("out0", c, "ab_out", N * c, N) for c in range(4)]
BLOCKS += [("v", c, "c_in", CV + N * c, N) for c in range(4)]
BLOCKS += [(k, c, "c_in", at + N * c, N) for k, at in (("q", CQ), ("k", CK)) for c in range(2)]
BLOCKS += [("r", c, "c_in", CR + N * c, N) for c in range(4)]
BLOCKS += [("out1", c, "c_out", N * c, N) for c in range(4)]
NB = len(BLOCKS)
POS = {(k, c): p for p, (k, c, _, _, _) in enumerate(BLOCKS, 1)}

_widths = [("ident", P), ("cosA", NT * 32), ("sinA", NT * 32), ("cosB", NT * 64), ("sinB", NT * 64),
           ("mask", 5 * CHUNK), ("tri", P), ("cum64", P), ("rev64", P), ("rev128", CHUNK), ("tail", P)]
CONST_AT, CONST_W = {}, 0
for _n, _w in _widths:
    CONST_AT[_n] = (CONST_W, CONST_W + _w)
    CONST_W += _w


def constants():
    t = np.zeros((P, CONST_W), np.float32)

    def put(name, a):
        lo, hi = CONST_AT[name]
        t[:, lo:hi] = a

    put("ident", np.eye(P))
    for name, half in (("A", A_HD // 2), ("B", B_HD // 2)):
        inv = np.float32(THETA) ** (-np.arange(half, dtype=np.float32) / np.float32(half))
        ang = np.arange(S, dtype=np.float32)[:, None] * inv[None, :].astype(np.float32)
        for f, fn in (("cos", np.cos), ("sin", np.sin)):
            put(f + name, fn(ang).reshape(NT, P, half).transpose(1, 0, 2).reshape(P, -1))
    row = np.arange(P)[:, None]
    col = np.arange(P)[None, :]
    m = np.zeros((P, 5, CHUNK), np.float32)
    m[CHUNK:, 0] = NEG
    m[:CHUNK, 4] = NEG
    put("mask", m.reshape(P, -1))
    put("tri", row <= col)
    same = row // CHUNK == col // CHUNK
    put("cum64", (row <= col) & same)
    put("rev64", (row > col) & same)
    put("rev128", (row > col)[:, :CHUNK])
    put("tail", np.where(col < CHUNK, (row > col) & same, row <= col))
    return t


TASKS = []


def _plan():
    add = TASKS.append

    def tiles(tag, kts=range(KT)):
        for kt in kts:
            add((f"{tag}{kt}", "dve"))

    tiles("x")
    add(("akT", "act"))
    for g in range(4):
        add((f"aqT{g}", "act"))
        for h in range(4 * g - 4, 4 * g) if g else ():
            add((f"SA{h}", "dve"))
    add(("bqT0", "act"))
    for h in range(12, 16):
        add((f"SA{h}", "dve"))
    for g in range(1, 4):
        add((f"bqT{g}", "act"))
    for g in range(4):
        add((f"bkT{g}", "act"))
    for m in range(B_MAPS):
        add((f"SB{m}", "dve"))
    for h in range(B_HEADS):
        add((f"PB{h}", "dve"))
    for h in range(B_HEADS):
        add((f"OB{h}", "act"))
    for h in range(A_HEADS):
        add((f"PA{h}", "act" if h % 2 else "dve"))
    tiles("y")
    tiles("h")
    add(("lr", "dve"))
    for t in range(NT):
        for c in range(2):
            add((f"z{t}{c}", "dve"))
    for name in ("cum0", "rev0", "far0", "cum1", "tail1"):
        for c in range(2):
            add((f"{name}{c}", "act"))
    for g in range(4):
        add((f"qeT{g}", "act"))
    for g in range(4):
        add((f"keT{g}", "dve" if g % 2 else "act"))
    for g in range(2):
        add((f"a0T{g}", "act"))
        add((f"w1T{g}", "dve"))
    add(("k0T", "act"))
    for h in range(C_HEADS):
        add((f"SC{h}", "dve"))
    for h in range(C_HEADS):
        for t in range(NT):
            add((f"OC{h}{t}", "dve" if t else "act"))
    tiles("u")


_plan()
TASK = {name: k for k, (name, _) in enumerate(TASKS)}
BANKS = 4

TURN = [(0, i + 1) for i in range(6)] + [(1, 2), (1, 3)]
TAKE = [(b + (j + 4) // HALVES, (j + 4) % HALVES) for b, j in TURN]
CHANGES = [("y", 1, POS["bg", 1]), ("h", 2, POS["out0", 3]), ("u", 3, POS["r", 3])]
TILES_AFTER = {(last + b, j): (tag, g, (2 * i, 2 * i + 1)) for tag, g, last in CHANGES for i, (b, j) in enumerate(TAKE)}

RESULT = [(slice(0, 1), slice(0, 3 * N)), (slice(1, 2), slice(0, 3 * N)), (slice(0, NT), slice(3 * N, D))]


def freed(k):
    return TASKS[k][1], sum(e == TASKS[k][1] for _, e in TASKS[:k + 1])


class Steps:

    def __init__(self, eng, sem):
        self.eng, self.sem, self.n = eng, sem, 0

    def did(self, ins):
        ins.then_inc(self.sem, 1)
        self.n += 1
        return self.n

    def wait(self, n=None):
        self.eng.wait_ge(self.sem, self.n if n is None else n)


def build(nc, x, consts, gains, bhg, chg, final_g, w_ab_in, w_ab_out, w_c_in, w_c_out, sinks, lams,
          gate2, gate_b, out):
    W = {"ab_in": w_ab_in, "ab_out": w_ab_out, "c_in": w_c_in, "c_out": w_c_out}
    with ExitStack() as ctx:
        def sb(name, shape, dt=F32):
            return ctx.enter_context(nc.sbuf_tensor(name, shape, dt))

        def sem(name):
            return ctx.enter_context(nc.semaphore(name))

        xres = sb("xres", [P, NT, D])
        xTh = sb("xTh", [P, KT, S], F32R)
        xTl = sb("xTl", [P, KT, S], F32R)
        raw = sb("raw", [P, UNITS, 4, N])
        wh = sb("wh", [P, SPLIT_RING, 2, N], F32R)
        wl = sb("wl", [P, SPLIT_RING, 2, N], F32R)
        cst = sb("cst", [P, CONST_W])
        rope = sb("rope", [P, 384])
        gain = sb("gain", [P, 4, KT])
        hg = sb("hg", [P, 2 + 4])
        sink = sb("sink", [P, A_HEADS])
        small = sb("small", [P, 400])
        tA = sb("tA", [P, NT, N])
        tB = sb("tB", [P, N])
        tC = sb("tC", [P, N])
        lrh = sb("lrh", [P, KT * C_RANK + 64], F32R)
        lrl = sb("lrl", [P, KT * C_RANK + 64], F32R)
        arena = sb("arena", [P, 18816])

        def area(at, *shape):
            a = arena[:, at:at + int(np.prod(shape))]
            if len(shape) == 1:
                return a
            names = "abcd"[:len(shape)]
            return a.rearrange(f"p ({' '.join(names)}) -> p {' '.join(names)}", **dict(zip(names[1:], shape[1:])))

        aq = area(0, NT, 1024)
        bqT = area(0, B_MAPS, S)
        bq = area(2048, NT, 1024)
        bk = area(4096, NT, 1024)
        pB = area(2048, B_MAPS, 384)
        bv = area(6144, NT, 1024)
        ya = area(8192, NT, 1024)
        aqT = area(10240, 8, S)
        bkT = area(10240, B_MAPS, S)
        pT = area(10240, 4, 384)
        pA = area(12288, A_HEADS, 320)
        yb = area(0, NT, 1024)
        junkB = area(18304, S)
        akT = area(17408, A_KV, S)
        av = area(17920, 3, P)
        akr = area(18304, NT, A_KV, 2, A_HD)
        lam_in = area(6144, 4, B_HD)
        junk0 = area(12288, D)
        junkO = area(18304, N)
        v = area(0, NT, D)
        zs = area(4096, NT, C_DKS)
        gs = area(6144, NT, C_DKS)
        g2 = area(8192, C_DKS)
        gb = area(9216, C_DKS)
        lrw = area(10240, KT * C_RANK)
        lrT = area(10496, S)
        qeT = area(4096, 8, S)
        keT = area(6144, 8, S)
        a0T = area(8192, 8, P)
        kkT = area(9216, 8, P)
        w1T = area(10240, 8, P)
        qe = area(11264, NT, C_DKS)
        ke = area(13312, NT, C_DKS)
        a0 = area(15360, C_DKS)
        k0 = area(16384, C_DKS)
        w1 = area(17408, C_DKS)
        att = area(11264, C_HEADS, 384)
        on = area(12800, NT, D)
        junkC = area(16896, N)
        fg = area(4096, D)

        def c_(name):
            return cst[:, CONST_AT[name][0]:CONST_AT[name][1]]

        ident = c_("ident")
        mask = c_("mask")
        mask_a1 = mask.rearrange("p (g c) -> p g c", c=CHUNK)[:, 0:5:2, :]
        mask_t0 = mask[:, 3 * CHUNK:5 * CHUNK]
        mask_b1 = mask[:, CHUNK:5 * CHUNK]
        tri = c_("tri").bitcast(U32)

        at = [0]

        def sm(*shape):
            n = int(np.prod(shape))
            a = small[:, at[0]:at[0] + n]
            at[0] += n
            assert at[0] <= 400
            return a.rearrange("p (a b) -> p a b", b=shape[1]) if len(shape) == 2 else a

        ssq = [sm(NT, 1), sm(NT, 4), sm(NT, 4)]
        ss, mean, root, tmp = (sm(NT) for _ in range(4))
        rstd = [sm(NT) for _ in range(3)]
        rq = sm(NT)
        mx_a, neg_a, sum_a, ex_a, r_a, es_a = (sm(NT, A_HEADS) for _ in range(6))
        mx_b, neg_b, sum_b, r_b = (sm(NT, B_MAPS) for _ in range(4))
        head = {k: [sm(4, NT) for _ in range(5)] for k in "BC"}
        lam_sum, lam_exp, lam = sm(2), sm(2), sm(1)

        acc = [[ctx.enter_context(nc.psum_tensor(f"acc{p}{t}", [P, N], F32)) for t in range(NT)] for p in range(2)]
        banks = [ctx.enter_context(nc.psum_tensor(f"task{i}", [P, N], F32)) for i in range(BANKS)]

        def bank(name):
            return banks[TASK[name] % BANKS]

        x_in = [sem(f"x_in{i}") for i in range(4)]
        consts_in, small_in, gate_in, fg_in = sem("consts_in"), sem("small_in"), sem("gate_in"), sem("fg_in")
        raw_in = [sem(f"raw_in{u}") for u in range(UNITS)]
        hi_done, lo_done = sem("hi_done"), sem("lo_done")
        half_used = sem("half_used")
        acc_free = sem("acc_free")
        task_ready = sem("task_ready")
        task_free = {"act": sem("task_free_act"), "dve": sem("task_free_dve")}
        xh_done = sem("xh_done")
        sq_done = sem("sq_done")
        head_sq = sem("head_sq")
        root_in, root_done = sem("root_in"), sem("root_done")
        sig_done = sem("sig_done")
        gain_ready = sem("gain_ready")
        lam_summed, lam_exped = sem("lam_summed"), sem("lam_exped")
        max_ready = sem("max_ready")
        exp_a_done, exp_b_done = sem("exp_a_done"), sem("exp_b_done")
        w_ready = sem("w_ready")
        pt_used = sem("pt_used")
        pv_free = sem("pv_free")
        lr_pad, lr_hi, lr_split = sem("lr_pad"), sem("lr_hi"), sem("lr_split")
        nz_ready, ln_done, gate_ready = sem("nz_ready"), sem("ln_done"), sem("gate_ready")
        ident_in, gain_in = sem("ident_in"), sem("gain_in")
        att_zero = sem("att_zero")
        tile_added = sem("tile_added")
        factor_ready = sem("factor_ready")
        fin = [sem(f"fin{i}") for i in range(3)]
        stored = sem("stored")
        act_step, dve_step = sem("act_step"), sem("dve_step")
        block = ctx.enter_context(nc.Block())

        def width_of(p):
            return BLOCKS[p - 1][4]

        def wait_free(eng, name):
            who, n = freed(TASK[name])
            eng.wait_ge(task_free[who], n)

        @block.sync
        def _(sp):
            xv = x.rearrange("o (t p) n -> (o p) t n", p=P)
            for i in range(4):
                sp.dma_start(xres[:, :, i * N:(i + 1) * N], xv[:, :, i * N:(i + 1) * N]).then_inc(x_in[i], 16)

            def load(matrix, first, width, p):
                rows = W[matrix].rearrange("o (u k p) n -> (o p) u k n", p=P, k=4)
                for u in range(UNITS):
                    if not isinstance(p, int):
                        sp.wait_ge(lo_done, (p - 2) * HALVES + (2 * u + 2))
                    cols = slice(first, first + width) if isinstance(first, int) else bass.ds(first, width)
                    sp.dma_start(raw[:, u, :, 0:width], rows[:, u, :, cols]).then_inc(raw_in[u], 16)

            load("ab_in", AK, 2 * A_KV * A_HD, 1)
            for kind, blocks in (("aq", 2), ("bq", 4), ("ag", 2), ("bv", 4), ("out0", 4), ("v", 4), ("q", 4), ("r", 4), ("out1", 4)):
                p0 = POS[kind, 0]
                _, _, matrix, col0, _ = BLOCKS[p0 - 1]
                with sp.Fori(0, blocks) as b:
                    load(matrix, b * N + col0, N, b + p0)
            ov = out.rearrange("o (t p) n -> (o p) t n", p=P)
            for i, (ts, cols) in enumerate(RESULT):
                sp.wait_ge(fin[i], NT if i == 2 else 1)
                sp.dma_start(ov[:, ts, cols], xres[:, ts, cols]).then_inc(stored, 16)
            sp.wait_ge(stored, 16 * len(RESULT))

        @block.gpsimd
        def _(pool):
            pool.dma_start(cst[:, P:], consts[:, P:]).then_inc(consts_in, 16)
            pool.dma_start(gain[:, 2, :], gains[1]).then_inc(small_in, 16)
            pool.dma_start(hg[:, 0:2], bhg).then_inc(small_in, 16)
            pool.dma_start(hg[:, 2:6], chg).then_inc(small_in, 16)
            pool.dma_start(sink[:, :], sinks.broadcast_to([P, A_HEADS])).then_inc(small_in, 16)
            for i in range(4):
                pool.dma_start(lam_in[:, i, :], lams[i].broadcast_to([P, B_HD])).then_inc(small_in, 16)
            for pad in (lrh, lrl):
                nc.gpsimd.memset(pad[:, KT * C_RANK:].bitcast(F32), 0.0).then_inc(lr_pad, 1)
            pool.wait_ge(task_ready, TASK[f"y{KT - 1}"] + 1)
            pool.dma_start(g2[0:C_RANK, :], gate2).then_inc(gate_in, 16)
            pool.dma_start(gb, gate_b.broadcast_to([P, C_DKS])).then_inc(gate_in, 16)
            pool.dma_start(lrw.rearrange("p (k r) -> p k r", r=C_RANK),
                           w_c_in.rearrange("o (k p) n -> (o p) k n", p=P)[:, :, CLR:CLR + C_RANK]).then_inc(gate_in, 16)
            pool.wait_ge(task_ready, TASK["keT0"] + 1)
            nc.gpsimd.memset(att, 0.0).then_inc(att_zero, 1)
            pool.wait_ge(task_ready, TASK[f"SC{C_HEADS - 1}"] + 1)
            pool.dma_start(fg, final_g.broadcast_to([P, D])).then_inc(fg_in, 16)

        @block.scalar
        def _(act):
            A = nc.scalar.activation
            steps = Steps(act, act_step)

            def halves(p, js, extra=None):
                w = width_of(p)
                for j in js:
                    n = (p - 1) * HALVES + j
                    if j % 2 == 0:
                        act.wait_ge(raw_in[j // 2], 16 * p)
                    if n >= SPLIT_RING:
                        act.wait_ge(half_used, n - SPLIT_RING + 1)
                    A(wh[:, j % SPLIT_RING, :, 0:w], raw[:, j // 2, 2 * (j % 2):2 * (j % 2) + 2, 0:w],
                      ACT.Copy).then_inc(hi_done, 1)
                    for _ in range(min(4, len(extra or ()))):
                        extra.pop(0)()
                    if (p, j) in TILES_AFTER:
                        stationary(*TILES_AFTER[p, j])

            def task(name):
                act.wait_ge(task_ready, TASK[name] + 1)
                return bank(name)

            def stationary(tag, g, kts):
                for kt in kts:
                    A(xTh[:, kt, :], task(f"{tag}{kt}")[:, 0:S], ACT.Copy, scale=gain[:, g, kt:kt + 1]).then_inc(xh_done, 1)

            squares = {"row": 0, "head": 0}

            def square(kind, junk, src, total):
                s = sq_done if kind == "row" else head_sq
                if squares[kind]:
                    act.wait_ge(s, squares[kind])
                A(junk, src, ACT.Square, accum_out=total).then_inc(s, 1)
                squares[kind] += 1

            roots = [0]

            def sqrt(dst, src):
                roots[0] += 1
                act.wait_ge(root_in, roots[0])
                A(dst, src, ACT.Sqrt).then_inc(root_done, 1)

            def sigmoid(p, k):
                gates = [q for q, b in enumerate(BLOCKS[:p - 1], 1) if b[0] in ("ag", "bg", "r")]
                if gates:
                    act.wait_ge(acc_free, gates[-1] + 1)
                act.wait_ge(half_used, HALVES * p)
                for t in range(NT):
                    A(tA[:, t, :], acc[p % 2][t][:, :], ACT.Sigmoid, scale=rstd[k][:, t:t + 1]).then_inc(sig_done, 1)

            def copy_out(name, dst):
                A(dst, task(name)[:, :].rearrange("p (a b) -> p a b", b=dst.shape[2]), ACT.Copy).then_inc(task_free["act"], 1)

            exps = []
            for m in range(B_MAPS):
                for t in range(NT):
                    def exp_b(m=m, t=t):
                        if (m, t) == (0, 0):
                            act.wait_ge(max_ready, 3)
                        cols = slice(0, P) if t == 0 else slice(P, 384)
                        A(pB[:, m, cols], pB[:, m, cols], ACT.Exp, bias=neg_b[:, t, m:m + 1], scale=B_HD ** -0.5,
                          accum_out=sum_b[:, t, m:m + 1]).then_inc(exp_b_done, 1)
                    exps.append(exp_b)
            for h in range(A_HEADS):
                for t in range(NT):
                    def exp_a(h=h, t=t):
                        cols = slice(0, P) if t == 0 else slice(P, 320)
                        A(pA[:, h, cols], pA[:, h, cols], ACT.Exp, bias=neg_a[:, t, h:h + 1], scale=A_HD ** -0.5,
                          accum_out=sum_a[:, t, h:h + 1]).then_inc(exp_a_done, 1)
                    exps.append(exp_a)
            exps.append(lambda: A(ex_a, es_a, ACT.Exp).then_inc(exp_a_done, 1))

            def head_norms(k, src, junk, width):
                out = []
                for h in range(4):
                    for t in range(NT):
                        def one(h=h, t=t):
                            if t == 0:
                                wait_free(act, f"O{k}{h}" if k == "B" else f"OC{h}1")
                            square("head", junk, src[:, t, h * width:(h + 1) * width], head[k][0][:, h, t:t + 1])
                        out.append(one)
                return out

            norms_b = head_norms("B", yb, junkB, 2 * B_HD)
            norms_c = head_norms("C", on, junkC, C_DV)

            def pt_out(name, n):
                b = task(name)
                if n >= 2 * B_HEADS:
                    act.wait_ge(pt_used, n - 2 * B_HEADS + 1)
                elif n >= B_HEADS:
                    act.wait_ge(task_ready, TASK[f"OB{n - B_HEADS}"] + 1)
                A(pT[:, n % 4, 0:S], b[:, 0:S], ACT.Copy)
                A(pT[0:CHUNK, n % 4, S:384], b[0:CHUNK, S:384], ACT.Copy).then_inc(task_free["act"], 1)

            def after_block(p):
                kind, c, _, _, _ = BLOCKS[p - 1]
                if kind == "kv":
                    sqrt(root, mean)
                elif kind in ("ag", "bg"):
                    sigmoid(p, 0)
                elif kind == "r":
                    sigmoid(p, 1)
                elif kind in ("out0", "out1"):
                    n = sum(b[0] in ("out0", "out1") for b in BLOCKS[:p])
                    for t in range(NT):
                        act.wait_ge(*((acc_free, p + 1) if t else (tile_added, n)))
                        square("row", junkO, xres[:, t, c * N:(c + 1) * N], ssq[1 if kind == "out0" else 2][:, t, c:c + 1])

            def take_scores():
                copy_out("akT", akT)
                for name, dst in (("aqT", aqT), ("bqT", bqT), ("bkT", bkT)):
                    for g in range(4):
                        copy_out(f"{name}{g}", dst[:, 2 * g:2 * g + 2, :])

            def take_values():
                for h in range(B_HEADS):
                    copy_out(f"OB{h}", yb[:, :, h * S:(h + 1) * S])
                for h in range(1, A_HEADS, 2):
                    pt_out(f"PA{h}", B_HEADS + h)

            def log_gates():
                for t in range(NT):
                    act.wait_ge(nz_ready, t + 1)
                    steps.did(A(gs[:, t, :], gs[:, t, :], ACT.Exp))
                for t in range(NT):
                    steps.wait(steps.n - NT + 1 + t)
                    A(gs[:, t, :], gs[:, t, :], ACT.Ln, bias=1.0).then_inc(ln_done, 1)

            def decays():
                s = 1.0 / GATE_TAU

                def exp(name, c, *dst, rows=P):
                    b = task(f"{name}{c}")
                    for i, (d, scale) in enumerate(dst):
                        ins = A(d[0:rows, c * N:(c + 1) * N], b[0:rows, :], ACT.Exp, scale=scale)
                    ins.then_inc(task_free["act"], 1)

                for name, dst, rows in (("cum0", ((qe[:, 0, :], s), (ke[:, 0, :], -s)), P), ("rev0", ((a0, s),), P),
                                        ("far0", ((k0, s),), CHUNK), ("cum1", ((qe[:, 1, :], s), (ke[:, 1, :], -s)), P),
                                        ("tail1", ((w1, s),), P)):
                    for c in range(2):
                        exp(name, c, *dst, rows=rows)

            def take_gla():
                for g in range(4):
                    copy_out(f"qeT{g}", qeT[:, 2 * g:2 * g + 2, :])
                for g in (0, 2):
                    copy_out(f"keT{g}", keT[:, 2 * g:2 * g + 2, :])
                for g in range(2):
                    b = task(f"a0T{g}")[:, :].rearrange("p (k c) -> p k c", c=P)
                    A(a0T[:, 4 * g:4 * g + 4, 0:CHUNK], b[:, :, 0:CHUNK], ACT.Copy)
                    A(kkT[:, 4 * g:4 * g + 4, CHUNK:P], b[:, :, CHUNK:P], ACT.Copy).then_inc(task_free["act"], 1)
                A(kkT[:, :, 0:CHUNK], task("k0T")[:, :].rearrange("p (k c) -> p k c", c=CHUNK), ACT.Copy).then_inc(task_free["act"], 1)
                for h in range(C_HEADS):
                    A(on[:, 0, h * C_DV:(h + 1) * C_DV], task(f"OC{h}0")[:, :], ACT.Copy).then_inc(task_free["act"], 1)

            act.dma_start(cst[:, 0:P], consts[:, 0:P]).then_inc(ident_in, 16)
            act.dma_start(gain[:, 0, :], gains[0]).then_inc(gain_in, 16)
            act.wait_ge(gain_in, 16)
            stationary("x", 0, range(4))
            halves(1, (0, 1))
            for j in range(2, HALVES):
                stationary("x", 0, (2 * j, 2 * j + 1))
                halves(1, (j,))
            for i in range(4):
                act.wait_ge(x_in[i], 16)
            for t in range(NT):
                square("row", junk0, xres[:, t, :], ssq[0][:, t, 0:1])
            for p in range(2, NB + 1):
                kind, c, _, _, _ = BLOCKS[p - 1]
                extra = {"bv": exps, "bg": norms_b, "r": norms_c}.get(kind)
                halves(p, range(4), extra if (kind, c) not in (("bv", 0), ("bg", 0), ("r", 0)) else None)
                after_block(p - 1)
                if (kind, c) == ("aq", 0):
                    act.wait_ge(lam_summed, 1)
                    A(lam_exp, lam_sum, ACT.Exp).then_inc(lam_exped, 1)
                if (kind, c) == ("bv", 0):
                    take_scores()
                if (kind, c) == ("bg", 0):
                    while exps:
                        exps.pop(0)()
                    take_values()
                if (kind, c) == ("v", 0):
                    sqrt(root, mean)
                if (kind, c) == ("v", 1):
                    act.wait_ge(gate_in, 48)
                    act.wait_ge(lr_pad, 1)
                    A(lrh[:, 0:KT * C_RANK], lrw, ACT.Copy).then_inc(lr_hi, 1)
                if (kind, c) == ("v", 3):
                    log_gates()
                if (kind, c) == ("q", 0):
                    decays()
                if (kind, c) == ("r", 0):
                    take_gla()
                halves(p, range(4, 8), extra)
                if (kind, c) in (("bg", 0), ("r", 0)):
                    k = "B" if kind == "bg" else "C"
                    sqrt(head[k][2], head[k][1])
            after_block(NB)
            sqrt(root, mean)
            act.wait_ge(factor_ready, roots[0])
            ts, cols = RESULT[1]
            A(xres[:, 1, cols], xres[:, 1, cols], ACT.Copy, scale=rstd[2][:, 1:2]).then_inc(fin[1], 1)

        @block.vector
        def _(dve):
            V = nc.vector
            steps = Steps(dve, dve_step)

            def halves(p, js, extra=None):
                w = width_of(p)
                for j in js:
                    dve.wait_ge(hi_done, (p - 1) * HALVES + j + 1)
                    V.tensor_tensor(wl[:, j % SPLIT_RING, :, 0:w], raw[:, j // 2, 2 * (j % 2):2 * (j % 2) + 2, 0:w],
                                    wh[:, j % SPLIT_RING, :, 0:w].bitcast(F32), ALU.subtract).then_inc(lo_done, 1)
                    if extra:
                        extra.pop(0)()
                    if (p, j) in TILES_AFTER:
                        stationary(*TILES_AFTER[p, j])

            def task(name):
                dve.wait_ge(task_ready, TASK[name] + 1)
                return bank(name)

            def emptied(ins):
                ins.then_inc(task_free["dve"], 1)

            highs = [0]

            def stationary(tag, g, kts):
                for kt in kts:
                    b = task(f"{tag}{kt}")
                    highs[0] += 1
                    dve.wait_ge(xh_done, highs[0])
                    emptied(V.scalar_tensor_tensor(out=xTl[:, kt, :], in0=b[:, 0:S], scalar=gain[:, g, kt:kt + 1],
                                                   in1=xTh[:, kt, :].bitcast(F32), op0=ALU.mult, op1=ALU.subtract))

            def then(ins):
                steps.did(ins)
                steps.wait()

            roots = [0]

            def rsqrt(dst, total, mean_, root_, tmp_, inv_n, eps):
                V.tensor_scalar(mean_, total, inv_n, eps, ALU.mult, ALU.add).then_inc(root_in, 1)
                roots[0] += 1
                dve.wait_ge(root_done, roots[0])
                then(V.reciprocal(dst, root_))
                then(V.tensor_tensor(tmp_, dst, dst, ALU.mult))
                then(V.tensor_tensor(tmp_, tmp_, mean_, ALU.mult))
                then(V.tensor_scalar(tmp_, tmp_, -0.5, 1.5, ALU.mult, ALU.add))
                V.tensor_tensor(dst, dst, tmp_, ALU.mult).then_inc(factor_ready, 1)
                dve.wait_ge(factor_ready, roots[0])

            def row_norm(k):
                total = ssq[k][:, :, 0]
                if k:
                    then(V.reduce_sum(ss, ssq[k], AX_X))
                    total = ss
                rsqrt(rstd[k], total, mean, root, tmp, 1.0 / D, NORM_EPS)

            def head_norms(k, width, n):
                def one():
                    dve.wait_ge(head_sq, n)
                    sq, mean_, root_, tmp_, r = head[k]
                    rsqrt(r, sq, mean_, root_, tmp_, 1.0 / width, HEAD_EPS)
                return [one]

            norms_b = head_norms("B", 2 * B_HD, NT * B_HEADS)
            norms_c = head_norms("C", C_DV, NT * (B_HEADS + C_HEADS))

            def rotate(src, dst, cos, sin):
                n, half = src.shape[1], src.shape[3]
                size = n * 2 * half
                b4 = tB[:, 0:size].rearrange("p (n a c) -> p n a c", a=2, c=half)
                c4 = tC[:, 0:size].rearrange("p (n a c) -> p n a c", a=2, c=half)
                cos_all = cos.unsqueeze(1).broadcast_to([P, 2 * n, half])
                sin_all = sin.unsqueeze(1).broadcast_to([P, n, half])
                steps.did(V.tensor_tensor(b4.rearrange("p n a c -> p (n a) c"), src.rearrange("p n a c -> p (n a) c"), cos_all, ALU.mult))
                steps.did(V.scalar_tensor_tensor(out=c4[:, :, 0, :], in0=src[:, :, 1, :], scalar=-1.0, in1=sin_all,
                                                 op0=ALU.mult, op1=ALU.mult))
                then(V.tensor_tensor(c4[:, :, 1, :], src[:, :, 0, :], sin_all, ALU.mult))
                return V.tensor_tensor(dst, b4, c4, ALU.add)

            def table(name, t):
                half, first = (32, 0) if name == "A" else (64, 128)
                cos = rope[:, first + t * half:first + (t + 1) * half]
                sin = rope[:, first + NT * half + t * half:first + NT * half + (t + 1) * half]
                return cos, sin

            def after_block(p):
                kind, c, _, _, _ = BLOCKS[p - 1]
                cols = slice(c * N, (c + 1) * N)
                dve.wait_ge(half_used, HALVES * p)
                o = acc[p % 2]
                if kind == "kv":
                    dve.wait_ge(sq_done, NT)
                    row_norm(0)
                    dve.wait_ge(consts_in, 16)
                    for t in range(NT):
                        for dst, src in zip(table("A", t) + table("B", t), ("cosA", "sinA", "cosB", "sinB")):
                            half = dst.shape[1]
                            steps.did(V.tensor_scalar(dst, c_(src)[:, t * half:(t + 1) * half], rstd[0][:, t:t + 1], None, ALU.mult))
                    steps.wait()
                    for t in range(NT):
                        cos, sin = table("A", t)
                        then(rotate(o[t][:, 0:P].rearrange("p (n a c) -> p n a c", n=A_KV, a=2),
                                    akr[:, t, :, 0, :].rearrange("p n (a c) -> p n a c", a=2), cos, sin))
                        steps.did(V.tensor_copy(akr[:, t, :, 1, :], akr[:, t, :, 0, :]))
                    for rows, src, kt in ((slice(0, P), (0, slice(0, P)), 0), (slice(0, CHUNK), (0, slice(CHUNK, P)), 1),
                                          (slice(CHUNK, P), (1, slice(0, CHUNK)), 1), (slice(0, CHUNK), (1, slice(CHUNK, P)), 2)):
                        ins = V.tensor_scalar(av[rows, kt, :], o[src[0]][src[1], P:2 * P], rstd[0][src[1], src[0]:src[0] + 1], None, ALU.mult)
                        if kt != 2:
                            steps.did(ins)
                elif kind in ("aq", "bq", "bk"):
                    name, dst = ("A", aq) if kind == "aq" else ("B", bq if kind == "bq" else bk)
                    for t in range(NT):
                        cos, sin = table(name, t)
                        shape = dict(a=2, c=cos.shape[1])
                        ins = rotate(o[t][:, :].rearrange("p (n a c) -> p n a c", **shape),
                                     dst[:, t, cols].rearrange("p (n a c) -> p n a c", **shape), cos, sin)
                        if t == 0:
                            then(ins)
                elif kind == "bv":
                    for t in range(NT):
                        ins = V.tensor_scalar(bv[:, t, cols], o[t][:, :], rstd[0][:, t:t + 1], None, ALU.mult)
                elif kind in ("ag", "bg", "r"):
                    n = sum(b[0] in ("ag", "bg", "r") for b in BLOCKS[:p])
                    r = rstd[1 if kind == "r" else 0]
                    for t in range(NT):
                        dve.wait_ge(sig_done, NT * (n - 1) + t + 1)
                        if kind == "ag":
                            ins = V.scalar_tensor_tensor(out=ya[:, t, cols], in0=o[t][:, :], scalar=r[:, t:t + 1],
                                                         in1=tA[:, t, :], op0=ALU.mult, op1=ALU.mult)
                        else:
                            then(V.scalar_tensor_tensor(out=tB[:, :], in0=o[t][:, :], scalar=r[:, t:t + 1],
                                                        in1=tA[:, t, :], op0=ALU.mult, op1=ALU.mult))
                            n_heads, k, y = (2, "B", yb) if kind == "bg" else (1, "C", on)
                            w = N // n_heads
                            for i in range(n_heads):
                                h = n_heads * c + i
                                y_h = y[:, t, h * w:(h + 1) * w]
                                ins = V.scalar_tensor_tensor(out=y_h, in0=y_h, scalar=head[k][4][:, h, t:t + 1],
                                                             in1=tB[:, i * w:(i + 1) * w], op0=ALU.mult, op1=ALU.mult)
                                if (t, i) != (NT - 1, n_heads - 1):
                                    then(ins)
                elif kind in ("out0", "out1"):
                    for t in range(NT):
                        ins = V.tensor_tensor(xres[:, t, cols], o[t][:, :], xres[:, t, cols], ALU.add)
                        if t == 0:
                            ins.then_inc(tile_added, 1)
                elif kind == "v":
                    for t in range(NT):
                        ins = V.tensor_scalar(v[:, t, cols], o[t][:, :], rstd[1][:, t:t + 1], None, ALU.mult)
                elif kind == "q":
                    if c == 0:
                        wait_free(dve, "tail11")
                    for t in range(NT):
                        steps.did(V.scalar_tensor_tensor(out=qe[:, t, cols], in0=o[t][:, :], scalar=rq[:, t:t + 1],
                                                         in1=qe[:, t, cols], op0=ALU.mult, op1=ALU.mult))
                    late = slice(CHUNK, P)
                    ins = V.scalar_tensor_tensor(out=w1[late, cols], in0=o[1][late, :], scalar=rq[late, 1:2],
                                                 in1=w1[late, cols], op0=ALU.mult, op1=ALU.mult)
                elif kind == "k":
                    early = slice(0, CHUNK)
                    for t in range(NT):
                        steps.did(V.scalar_tensor_tensor(out=ke[:, t, cols], in0=o[t][:, :], scalar=rstd[1][:, t:t + 1],
                                                         in1=ke[:, t, cols], op0=ALU.mult, op1=ALU.mult))
                    steps.did(V.scalar_tensor_tensor(out=a0[:, cols], in0=o[0][:, :], scalar=rstd[1][:, 0:1],
                                                     in1=a0[:, cols], op0=ALU.mult, op1=ALU.mult))
                    steps.did(V.scalar_tensor_tensor(out=k0[early, cols], in0=o[0][early, :], scalar=rstd[1][early, 0:1],
                                                     in1=k0[early, cols], op0=ALU.mult, op1=ALU.mult))
                    ins = V.scalar_tensor_tensor(out=w1[early, cols], in0=o[1][early, :], scalar=rstd[1][early, 1:2],
                                                 in1=w1[early, cols], op0=ALU.mult, op1=ALU.mult)
                ins.then_inc(acc_free, 1)

            def masked(name, out_, src, mask_, total):
                return V.tensor_tensor_reduce(out=out_, in0=src, in1=mask_, scale=1.0, scalar=-3.0e38, op0=ALU.add,
                                              op1=ALU.max, accum_out=total)

            def take_scores():
                g3 = dict(c=CHUNK)
                for h in range(A_HEADS):
                    b = task(f"SA{h}")
                    steps.did(masked("A", pA[:, h, 0:P], b[:, 0:P], mask_t0, mx_a[:, 0, h:h + 1]))
                    emptied(masked("A", pA[:, h, P:320].rearrange("p (g c) -> p g c", **g3),
                                   b[:, P:320].rearrange("p (g c) -> p g c", **g3), mask_a1, mx_a[:, 1, h:h + 1]))
                for m in range(B_MAPS):
                    b = task(f"SB{m}")
                    steps.did(masked("B", pB[:, m, 0:P], b[:, 0:P], mask_t0, mx_b[:, 0, m:m + 1]))
                    emptied(masked("B", pB[:, m, P:384], b[:, P:384], mask_b1, mx_b[:, 1, m:m + 1]))
                steps.wait()
                wait_free(dve, f"SB{B_MAPS - 1}")
                then(V.scalar_tensor_tensor(out=es_a, in0=mx_a, scalar=A_HD ** -0.5,
                                            in1=sink[:, :].unsqueeze(1).broadcast_to([P, NT, A_HEADS]), op0=ALU.mult, op1=ALU.max))
                V.tensor_scalar(neg_a, es_a, -1.0, None, ALU.mult).then_inc(max_ready, 1)
                dve.wait_ge(max_ready, 1)
                V.tensor_tensor(es_a, sink[:, :].unsqueeze(1).broadcast_to([P, NT, A_HEADS]), neg_a, ALU.add).then_inc(max_ready, 1)
                V.tensor_scalar(neg_b, mx_b, -(B_HD ** -0.5), None, ALU.mult).then_inc(max_ready, 1)

            jobs = []
            for h in range(B_HEADS):
                for t in range(NT):
                    def differ(h=h, t=t):
                        if (h, t) == (0, 0):
                            dve.wait_ge(exp_b_done, NT * B_MAPS)
                            then(V.reciprocal(r_b, sum_b))
                            odd = r_b[:, :, 1:B_MAPS:2]
                            then(V.tensor_scalar(odd, odd, lam, None, ALU.mult))
                        cols = slice(0, P) if t == 0 else slice(P, 384)
                        w = cols.stop - cols.start
                        then(V.tensor_scalar(tC[:, 0:w], pB[:, 2 * h + 1, cols], r_b[:, t, 2 * h + 1:2 * h + 2], None, ALU.mult))
                        V.scalar_tensor_tensor(out=pB[:, 2 * h, cols], in0=pB[:, 2 * h, cols], scalar=r_b[:, t, 2 * h:2 * h + 1],
                                               in1=tC[:, 0:w], op0=ALU.mult, op1=ALU.subtract).then_inc(w_ready, 1)
                        dve.wait_ge(w_ready, NT * h + t + 1)
                    jobs.append(differ)

            def pt_out(name, n):
                b = task(name)
                if n >= 2 * B_HEADS:
                    dve.wait_ge(pt_used, n - 2 * B_HEADS + 1)
                elif n >= B_HEADS:
                    dve.wait_ge(task_ready, TASK[f"OB{n - B_HEADS}"] + 1)
                if n >= B_HEADS:
                    V.tensor_copy(pT[:, n % 4, 0:S], b[:, 0:S])
                    emptied(V.tensor_copy(pT[0:CHUNK, n % 4, S:384], b[0:CHUNK, S:384]))
                else:
                    emptied(V.tensor_copy(pT[:, n % 4, :], b[:, 0:384]))

            def take_values():
                for h in range(B_HEADS):
                    pt_out(f"PB{h}", h)
                for h in range(0, A_HEADS, 2):
                    pt_out(f"PA{h}", B_HEADS + h)
                dve.wait_ge(exp_a_done, NT * A_HEADS + 1)
                then(V.tensor_tensor(r_a, sum_a, ex_a, ALU.add))
                then(V.reciprocal(r_a, r_a))
                for g in range(A_KV):
                    dve.wait_ge(pt_used, A_GROUP * (g + 1))
                    for t in range(NT):
                        then(V.tensor_tensor(tB[:, :].rearrange("p (h d) -> p h d", d=A_HD),
                                             acc[g][t][:, :].rearrange("p (h d) -> p h d", d=A_HD),
                                             r_a[:, t, g * A_GROUP:(g + 1) * A_GROUP].unsqueeze(2).broadcast_to([P, A_GROUP, A_HD]),
                                             ALU.mult))
                        y = ya[:, t, g * N:(g + 1) * N]
                        V.tensor_tensor(y, y, tB[:, :], ALU.mult).then_inc(pv_free, 1)
                        dve.wait_ge(pv_free, NT * g + t + 1)

            def take_gate_inputs():
                dve.wait_ge(gate_in, 48)
                for t in range(NT):
                    for c in range(2):
                        cols = slice(c * N, (c + 1) * N)
                        emptied(V.scalar_tensor_tensor(out=zs[:, t, cols], in0=task(f"z{t}{c}")[:, :], scalar=rstd[1][:, t:t + 1],
                                                       in1=gb[:, cols], op0=ALU.mult, op1=ALU.add))
                    wait_free(dve, f"z{t}1")
                    V.scalar_tensor_tensor(out=gs[:, t, :], in0=zs[:, t, :], scalar=-1.0, in1=zs[:, t, :],
                                           op0=ALU.mult, op1=ALU.min).then_inc(nz_ready, 1)

            def log_sigmoid():
                for t in range(NT):
                    dve.wait_ge(ln_done, t + 1)
                    V.scalar_tensor_tensor(out=gs[:, t, :], in0=zs[:, t, :], scalar=0.0, in1=gs[:, t, :],
                                           op0=ALU.min, op1=ALU.subtract).then_inc(gate_ready, 1)

            def take_gla():
                for g in (1, 3):
                    emptied(V.tensor_copy(keT[:, 2 * g:2 * g + 2, :], task(f"keT{g}")[:, :].rearrange("p (k c) -> p k c", c=S)))
                for g in range(2):
                    emptied(V.tensor_copy(w1T[:, 4 * g:4 * g + 4, :], task(f"w1T{g}")[:, :].rearrange("p (k c) -> p k c", c=P)))
                dve.wait_ge(att_zero, 1)
                for h in range(C_HEADS):
                    b = task(f"SC{h}")
                    for t in range(NT):
                        steps.did(V.copy_predicated(att[:, h, t * P:(t + 1) * P], tri, b[:, t * P:(t + 1) * P]))
                    emptied(V.tensor_copy(att[:, h, S:384], b[:, S:384]))
                for h in range(C_HEADS):
                    emptied(V.tensor_copy(on[:, 1, h * C_DV:(h + 1) * C_DV], task(f"OC{h}1")[:, :]))

            def final_gain(c):
                dve.wait_ge(fg_in, 16)
                dve.wait_ge(sq_done, NT * (1 + 4 + c + 1))
                cols = slice(c * N, (c + 1) * N)
                return V.tensor_tensor(xres[:, :, cols], xres[:, :, cols],
                                       fg[:, cols].unsqueeze(1).broadcast_to([P, NT, N]), ALU.mult)

            V.memset(small[:, 399:400], 0.0).then_inc(acc_free, 1)
            stationary("x", 0, range(4))
            halves(1, (0, 1))
            for j in range(2, HALVES):
                stationary("x", 0, (2 * j, 2 * j + 1))
                halves(1, (j,))

            def prepare():
                dve.wait_ge(small_in, 8 * 16)
                steps.did(V.memset(gain[:, 1, 0:8], 1.0))
                steps.did(V.tensor_scalar(gain[:, 1, 8:16].rearrange("p (h k) -> p h k", k=2),
                                          hg[:, 0:2].unsqueeze(1).broadcast_to([P, B_HEADS, 2]), 1.0 - LAMBDA_INIT, None, ALU.mult))
                V.tensor_copy(gain[:, 3, :].rearrange("p (h k) -> p h k", k=4),
                              hg[:, 2:6].unsqueeze(1).broadcast_to([P, C_HEADS, 4])).then_inc(gain_ready, 1)
                for i in range(2):
                    ins = V.tensor_tensor_reduce(out=tB[:, i * B_HD:(i + 1) * B_HD], in0=lam_in[:, 2 * i, :], in1=lam_in[:, 2 * i + 1, :],
                                                 scale=1.0, scalar=0.0, op0=ALU.mult, op1=ALU.add, accum_out=lam_sum[:, i:i + 1])
                    if i == 0:
                        then(ins)
                ins.then_inc(lam_summed, 1)
                dve.wait_ge(lam_exped, 1)
                then(V.tensor_tensor(lam, lam_exp[:, 0:1], lam_exp[:, 1:2], ALU.subtract))
                then(V.tensor_scalar(lam, lam, LAMBDA_INIT, None, ALU.add))

            for p in range(2, NB + 1):
                kind, c, _, _, _ = BLOCKS[p - 1]
                extra = {("bv", 1): jobs, ("bg", 0): norms_b, ("r", 0): norms_c}.get((kind, c))
                halves(p, range(4), extra if kind == "bv" else None)
                after_block(p - 1)
                if (kind, c) == ("aq", 0):
                    prepare()
                if (kind, c) == ("bv", 0):
                    take_scores()
                if (kind, c) == ("bg", 0):
                    assert not jobs
                    take_values()
                if (kind, c) == ("v", 0):
                    dve.wait_ge(sq_done, NT * (1 + 4))
                    row_norm(1)
                    then(V.tensor_scalar(rq, rstd[1], C_DK ** -0.5, None, ALU.mult))
                if (kind, c) == ("v", 1):
                    dve.wait_ge(lr_hi, 1)
                    V.tensor_tensor(lrl[:, 0:KT * C_RANK], lrw, lrh[:, 0:KT * C_RANK].bitcast(F32), ALU.subtract).then_inc(lr_split, 1)
                if (kind, c) == ("v", 2):
                    emptied(V.tensor_copy(lrT[0:C_RANK, :], task("lr")[0:C_RANK, 0:S]))
                if (kind, c) == ("v", 3):
                    take_gate_inputs()
                if (kind, c) == ("r", 0):
                    take_gla()
                if kind == "out1" and c >= 2:
                    steps.did(final_gain(c - 2))
                halves(p, range(4, 8), extra if kind == "bv" else None)
                if extra and kind != "bv":
                    extra.pop(0)()
                if (kind, c) == ("v", 3):
                    log_sigmoid()
            after_block(NB)
            steps.did(final_gain(2))
            dve.wait_ge(sq_done, NT * (1 + 4 + 4))
            row_norm(2)
            ts, cols = RESULT[0]
            V.tensor_scalar(xres[:, 0, cols], xres[:, 0, cols], rstd[2][:, 0:1], None, ALU.mult).then_inc(fin[0], 1)
            for t in range(NT):
                last = xres[:, t, 3 * N:D]
                V.scalar_tensor_tensor(out=last, in0=last, scalar=rstd[2][:, t:t + 1], in1=fg[:, 3 * N:D],
                                       op0=ALU.mult, op1=ALU.mult).then_inc(fin[2], 1)

        @block.tensor
        def _(pe):
            MM = nc.tensor.matmul

            def half(p, j, par, w, tag):
                pe.wait_ge(lo_done, p * HALVES + (j + 1 - HALVES))
                wait_free(pe, f"{tag}{2 * j + 1}")
                for kt in (2 * j, 2 * j + 1):
                    high, low = (a[:, j % SPLIT_RING, kt % 2, 0:w] for a in (wh, wl))
                    for t in range(NT):
                        o = acc[par][t][:, 0:w]
                        tokens = slice(t * P, (t + 1) * P)
                        MM(o, xTh[:, kt, tokens], high, start=kt == 0, stop=False)
                        MM(o, xTh[:, kt, tokens], low, start=False, stop=False)
                        ins = MM(o, xTl[:, kt, tokens], high, start=False, stop=kt == KT - 1)
                ins.then_inc(half_used, 1)

            def one_block(p, par, tag, w=N, between=None):
                if not isinstance(p, int) or p > 1:
                    pe.wait_ge(acc_free, p - 1)
                for j in range(HALVES):
                    half(p, j, par, w, tag)
                    if between and j in between:
                        between[j]()

            def pairs(kind, n, tag):
                p0 = POS[kind, 0]
                with pe.Fori(0, n) as i:
                    for k in range(2):
                        one_block(i * 2 + (p0 + k), (p0 + k) % 2, tag)

            def blocks(kind, cs, tag, between=None):
                for c in cs:
                    p = POS[kind, c]
                    one_block(p, p % 2, tag, between=(between or {}).get(c))

            def begin(name):
                k = TASK[name]
                if k >= BANKS:
                    wait_free(pe, TASKS[k - BANKS][0])
                return bank(name)

            def done(ins):
                ins.then_inc(task_ready, 1)

            def turn(name, sources, rows=P):
                b = begin(name)
                for i, s in enumerate(sources):
                    ins = nc.tensor.transpose(b[:, i * rows:(i + 1) * rows], s, ident[0:rows, 0:rows])
                done(ins)

            def turns(tag, kts):
                for kt in kts:
                    c = kt // 4
                    if tag == "y" and kt < 8:
                        src, k = ya, kt
                        pe.wait_ge(pv_free, NT * A_KV)
                    elif tag == "y":
                        src, k = yb, kt - 8
                        pe.wait_ge(acc_free, POS["bg", c - 2] + 1)
                    elif tag == "h":
                        src, k = xres, kt
                        pe.wait_ge(acc_free, POS["out0", c] + 1)
                    elif tag == "u":
                        src, k = on, kt
                        pe.wait_ge(acc_free, POS["r", c] + 1)
                    else:
                        src, k = xres, kt
                        pe.wait_ge(x_in[c], 16)
                    turn(f"{tag}{kt}", [src[:, t, k * P:(k + 1) * P] for t in range(NT)])

            def change(tag, which):
                def job(i):
                    return lambda: turns(tag, (2 * i, 2 * i + 1))
                return {j: job(i) for i, (b, j) in enumerate(TURN) if b == which}

            pe.wait_ge(ident_in, 16)
            turns("x", range(4))
            one_block(1, 1, "x", width_of(1),
                      {j: (lambda j=j: turns("x", (2 * j + 4, 2 * j + 5))) for j in range(6)})
            pe.wait_ge(consts_in, 16)
            pairs("aq", 4, "x")

            turn("akT", [akr[:, t, g, :, :].rearrange("p a d -> p (a d)") for g in range(A_KV) for t in range(NT)])

            def turn_heads(name, g, src):
                turn(f"{name}{g}", [src[:, t, h * P:(h + 1) * P] for h in (2 * g, 2 * g + 1) for t in range(NT)])

            def scores_a(h):
                b = begin(f"SA{h}")
                wait_free(pe, f"aqT{h // 4}")
                rows = slice(A_HD * (h % 2), A_HD * (h % 2) + A_HD)
                MM(b[:, 0:P], aqT[rows, h // 2, 0:P], akT[rows, h // A_GROUP, 0:P], start=True, stop=True)
                done(MM(b[:, P:320], aqT[rows, h // 2, P:S], akT[rows, h // A_GROUP, CHUNK:S], start=True, stop=True))

            for g in range(4):
                turn_heads("aqT", g, aq)
                if g:
                    for h in range(4 * g - 4, 4 * g):
                        scores_a(h)
            for g in range(4):
                turn_heads("bqT", g, bq)
                if g == 0:
                    for h in range(12, 16):
                        scores_a(h)
            for g in range(4):
                turn_heads("bkT", g, bk)
            for m in range(B_MAPS):
                b = begin(f"SB{m}")
                wait_free(pe, f"bkT{m // 2}")
                MM(b[:, 0:P], bqT[:, m, 0:P], bkT[:, m, 0:P], start=True, stop=True)
                done(MM(b[:, P:384], bqT[:, m, P:S], bkT[:, m, :], start=True, stop=True))

            blocks("bv", range(2), "x")

            for h in range(B_HEADS):
                pe.wait_ge(w_ready, NT * (h + 1))
                turn(f"PB{h}", [pB[:, 2 * h, i * P:(i + 1) * P] for i in range(3)])
            pe.wait_ge(acc_free, POS["bv", 1] + 1)
            for h in range(B_HEADS):
                b = begin(f"OB{h}")
                wait_free(pe, f"PB{h}")
                slot, cols = pT[:, h % 4, :], slice(h * S, (h + 1) * S)
                MM(b[:, 0:S], slot[:, 0:P], bv[:, 0, cols], start=True, stop=True)
                MM(b[:, S:2 * S], slot[:, P:S], bv[:, 0, cols], start=True, stop=False)
                done(MM(b[:, S:2 * S], slot[:, S:384], bv[:, 1, cols], start=False, stop=True))

            def values_a(h):
                wait_free(pe, f"PA{h}")
                g, slot = h // A_GROUP, pT[:, (B_HEADS + h) % 4, :]
                cols = slice((h % A_GROUP) * A_HD, (h % A_GROUP + 1) * A_HD)
                vals = av[:, :, g * A_HD:(g + 1) * A_HD]
                MM(acc[g][0][:, cols], slot[:, 0:P], vals[:, 0, :], start=True, stop=True)
                MM(acc[g][1][:, cols], slot[:, P:S], vals[:, 1, :], start=True, stop=False)
                MM(acc[g][1][:, cols], slot[0:CHUNK, S:384], vals[0:CHUNK, 2, :], start=False, stop=True).then_inc(pt_used, 1)

            pe.wait_ge(exp_a_done, NT * A_HEADS)
            ahead = 2
            for h in range(A_HEADS + ahead):
                if h < A_HEADS:
                    b = begin(f"PA{h}")
                    nc.tensor.transpose(b[:, 0:P], pA[:, h, 0:P], ident)
                    nc.tensor.transpose(b[:, P:S], pA[:, h, P:S], ident)
                    done(nc.tensor.transpose(b[0:CHUNK, S:384], pA[:, h, S:320], ident))
                if h >= ahead:
                    values_a(h - ahead)
            pe.wait_ge(pv_free, NT * A_KV)
            blocks("bg", range(2), "x", {1: change("y", 0)})

            blocks("out0", range(4), "y", {0: change("y", 1), 3: change("h", 0)})

            blocks("v", range(2), "h", {0: change("h", 1)})
            pe.wait_ge(lr_split, 1)
            pe.wait_ge(lr_pad, 2)
            b = begin("lr")
            for kt in range(KT):
                cols = slice(C_RANK * kt, C_RANK * kt + 80)
                for i, (wgt, a) in enumerate(((lrh, xTh), (lrh, xTl), (lrl, xTh))):
                    ins = MM(b[0:80, 0:S], wgt[:, cols], a[:, kt, :], start=kt + i == 0, stop=kt == KT - 1 and i == 2)
            done(ins)
            blocks("v", (2,), "h")
            wait_free(pe, "lr")
            pe.wait_ge(gate_in, 48)
            for t in range(NT):
                for c in range(2):
                    done(MM(begin(f"z{t}{c}")[:, :], lrT[0:C_RANK, t * P:(t + 1) * P], g2[0:C_RANK, c * N:(c + 1) * N],
                            start=True, stop=True))
            blocks("v", (3,), "h")
            pe.wait_ge(gate_ready, NT)
            for name, t, mat, rows in (("cum0", 0, "cum64", P), ("rev0", 0, "rev64", P), ("far0", 0, "rev128", CHUNK),
                                       ("cum1", 1, "cum64", P), ("tail1", 1, "tail", P)):
                for c in range(2):
                    done(MM(begin(f"{name}{c}")[0:rows, :], c_(mat), gs[:, t, c * N:(c + 1) * N], start=True, stop=True))
            pairs("q", 2, "h")

            for g in range(4):
                turn_heads("qeT", g, qe)
            pe.wait_ge(acc_free, POS["k", 1] + 1)
            for g in range(4):
                turn_heads("keT", g, ke)
            for g in range(2):
                for name, src in (("a0T", a0), ("w1T", w1)):
                    turn(f"{name}{g}", [src[:, k * P:(k + 1) * P] for k in range(4 * g, 4 * g + 4)])
            turn("k0T", [k0[0:CHUNK, k * P:(k + 1) * P] for k in range(8)], rows=CHUNK)
            wait_free(pe, "w1T1")
            wait_free(pe, "k0T")
            for h in range(C_HEADS):
                b = begin(f"SC{h}")
                ks = (2 * h, 2 * h + 1)
                for t in range(NT):
                    first = t * P
                    for i, k in enumerate(ks):
                        MM(b[:, first:first + P], keT[:, k, first:first + P], qeT[:, k, first:first + P], start=i == 0, stop=i == 1)
                    decayed = a0T if t == 0 else w1T
                    for i, k in enumerate(ks):
                        MM(b[0:CHUNK, first + CHUNK:first + P], decayed[:, k, 0:CHUNK], qeT[:, k, first + CHUNK:first + P],
                           start=i == 0, stop=i == 1)
                for i, k in enumerate(ks):
                    MM(b[:, S:S + CHUNK], kkT[:, k, :], qeT[:, k, P:P + CHUNK], start=i == 0, stop=i == 1)
                for i, k in enumerate(ks):
                    ins = MM(b[:, S + CHUNK:384], kkT[:, k, :], w1T[:, k, CHUNK:P], start=i == 0, stop=i == 1)
                done(ins)
            for h in range(C_HEADS):
                cols = slice(h * C_DV, (h + 1) * C_DV)
                b = begin(f"OC{h}0")
                wait_free(pe, f"SC{h}")
                done(MM(b[:, :], att[:, h, 0:P], v[:, 0, cols], start=True, stop=True))
                b = begin(f"OC{h}1")
                MM(b[:, :], att[:, h, S:384], v[:, 0, cols], start=True, stop=False)
                done(MM(b[:, :], att[:, h, P:S], v[:, 1, cols], start=False, stop=True))
            blocks("r", range(4), "h", {3: change("u", 0)})
            blocks("out1", range(4), "u", {0: change("u", 1)})


def kernel(**inputs):
    import concourse.bacc as bacc
    from concourse.bass_utils import run_bass_kernel_spmd

    a = {k: np.ascontiguousarray(i) for k, i in inputs.items()}
    arrays = {
        "x": a["x"],
        "consts": constants(),
        "norm_g": np.ascontiguousarray(a["norm_g"].reshape(2, KT, P).transpose(0, 2, 1)),
        "b_head_g": np.ascontiguousarray(a["b_head_g"].reshape(2, P).T),
        "c_head_g": np.ascontiguousarray(a["c_head_g"].reshape(4, P).T),
        "final_g": a["final_g"].reshape(1, D),
        "ab_w_in": a["ab_w_in"], "ab_w_out": a["ab_w_out"], "c_w_in": a["c_w_in"], "c_w_out": a["c_w_out"],
        "a_sinks": a["a_sinks"], "lq1": a["b_lq1"], "lk1": a["b_lk1"], "lq2": a["b_lq2"], "lk2": a["b_lk2"],
        "gate2": a["c_w_gate2"].reshape(C_RANK, C_DKS), "gate_b": a["c_gate_b"].reshape(1, C_DKS),
    }
    nc = bacc.Bacc("TRN2", target_bir_lowering=False, num_devices=1)
    d = {k: nc.dram_tensor(f"in_{k}", i.shape, mybir.dt.from_np(i.dtype), kind="ExternalInput").ap() for k, i in arrays.items()}
    out = nc.dram_tensor("out", (1, S, D), F32, kind="ExternalOutput").ap()
    build(nc, d["x"], d["consts"], [d["norm_g"][i] for i in range(2)], d["b_head_g"], d["c_head_g"], d["final_g"],
          d["ab_w_in"], d["ab_w_out"], d["c_w_in"], d["c_w_out"], d["a_sinks"],
          [d[k] for k in ("lq1", "lk1", "lq2", "lk2")], d["gate2"], d["gate_b"], out)
    r = run_bass_kernel_spmd(nc, [{f"in_{k}": i for k, i in arrays.items()}], core_ids=[0])
    return r.results[0]["out"]
```
